# Optimizing a Trainium2 kernel written in Bass

```python
import jax, jax.numpy as jnp
from jax import lax
import numpy as np
import jax
import jax.numpy as jnp

D_MODEL = 1024
BATCH = 1
SEQ = 512
DEPTH = 2

MIX_WIDTH = 2 * D_MODEL
HEAD_DIM = 64
BLOCK = 128
SWA_HEADS = (MIX_WIDTH // 4) // HEAD_DIM
SWA_KV_HEADS = SWA_HEADS // 4
SWA_WINDOW = 128
FOX_HEADS = (MIX_WIDTH // 4) // HEAD_DIM
SSM_HEAD_DIM = 64
SSM_HEADS = (MIX_WIDTH // 2) // SSM_HEAD_DIM
SSM_GROUPS = 2
SSM_STATE = 128
SSM_CONV = 4
SSM_CHUNK = 128
MEM_TOKENS = 256
MEM_HEADS = 4
MEM_HEAD_DIM = D_MODEL // MEM_HEADS
ROPE_THETA = 10000.0
EPS = 1e-6
NEG_INF = -1e30

SWA_W = SWA_HEADS * HEAD_DIM
SWA_KV_W = SWA_KV_HEADS * HEAD_DIM
FOX_W = FOX_HEADS * HEAD_DIM
SSM_W = SSM_HEADS * SSM_HEAD_DIM
SSM_BC_W = SSM_GROUPS * SSM_STATE
SSM_CONV_W = SSM_W + 2 * SSM_BC_W
IN_SPLITS = (SWA_W, SWA_KV_W, SWA_KV_W, SWA_W,
             FOX_W, FOX_W, FOX_W, FOX_HEADS, FOX_W,
             SSM_W, SSM_CONV_W, SSM_HEADS)
IN_W = SWA_W + 2 * SWA_KV_W + SWA_W + 4 * FOX_W + FOX_HEADS + SSM_W + SSM_CONV_W + SSM_HEADS


def _offsets(sizes):
    out, acc = [], 0
    for s in sizes[:-1]:
        acc += s
        out.append(acc)
    return out

def rms_norm(x, w):
    xf = x.astype(jnp.float32)
    y = xf * lax.rsqrt(jnp.mean(xf * xf, axis=-1, keepdims=True) + EPS)
    return (y * w.astype(jnp.float32)).astype(x.dtype)

def rope_tables(seq):
    pos = jnp.arange(seq, dtype=jnp.float32)
    inv = 1.0 / (ROPE_THETA ** (jnp.arange(0, HEAD_DIM, 2, dtype=jnp.float32) / HEAD_DIM))
    ang = pos[:, None] * inv[None, :]
    return jnp.cos(ang), jnp.sin(ang)

def apply_rope(x, cos, sin):
    xf = x.astype(jnp.float32)
    x1, x2 = jnp.split(xf, 2, axis=-1)
    c = cos[None, :, None, :]
    s = sin[None, :, None, :]
    return jnp.concatenate([x1 * c - x2 * s, x2 * c + x1 * s], axis=-1).astype(x.dtype)

def sliding_window_attention(q, k, v, sinks):
    b, s, hq, hd = q.shape
    hkv = k.shape[2]
    g = hq // hkv
    n = s // BLOCK
    qb = q.reshape(b, n, BLOCK, hkv, g, hd)
    kb = k.reshape(b, n, BLOCK, hkv, hd)
    vb = v.reshape(b, n, BLOCK, hkv, hd)
    pad = ((0, 0), (1, 0), (0, 0), (0, 0), (0, 0))
    kcat = jnp.concatenate([jnp.pad(kb, pad)[:, :-1], kb], axis=2)
    vcat = jnp.concatenate([jnp.pad(vb, pad)[:, :-1], vb], axis=2)
    scores = jnp.einsum('bnqkgd,bnskd->bnkgqs', qb, kcat).astype(jnp.float32) * (hd ** -0.5)
    qi = jnp.arange(BLOCK)[:, None]
    si = jnp.arange(2 * BLOCK)[None, :] - BLOCK
    rel = qi - si
    band = (rel >= 0) & (rel < SWA_WINDOW)
    valid = (jnp.arange(n)[:, None, None] * BLOCK + si[None]) >= 0
    mask = band[None] & valid
    scores = jnp.where(mask[None, :, None, None], scores, NEG_INF)
    sink = sinks.astype(jnp.float32).reshape(hkv, g)[None, None, :, :, None, None]
    m = jnp.maximum(jnp.max(scores, axis=-1, keepdims=True), sink)
    p = jnp.exp(scores - m)
    probs = (p / (jnp.sum(p, axis=-1, keepdims=True) + jnp.exp(sink - m))).astype(v.dtype)
    out = jnp.einsum('bnkgqs,bnskd->bnqkgd', probs, vcat)
    return out.reshape(b, s, hq, hd)

def forgetting_attention(q, k, v, log_f):
    b, s, h, hd = q.shape
    n = s // BLOCK
    c = jnp.cumsum(log_f, axis=1).transpose(0, 2, 1)
    qb = q.reshape(b, n, BLOCK, h, hd).swapaxes(0, 1)
    cq = c.reshape(b, h, n, BLOCK).transpose(2, 0, 1, 3)
    kpos = jnp.arange(s)
    scale = hd ** -0.5

    def one_block(args):
        qi, ci, i = args
        logits = jnp.einsum('bqhd,bkhd->bhqk', qi, k).astype(jnp.float32) * scale
        logits = logits + ci[..., :, None] - c[:, :, None, :]
        qpos = i * BLOCK + jnp.arange(BLOCK)
        mask = kpos[None, :] <= qpos[:, None]
        logits = jnp.where(mask, logits, NEG_INF)
        probs = jax.nn.softmax(logits, axis=-1).astype(v.dtype)
        return jnp.einsum('bhqk,bkhd->bqhd', probs, v)

    out = lax.map(one_block, (qb, cq, jnp.arange(n)))
    return out.swapaxes(0, 1).reshape(b, s, h, hd)

def causal_depthwise_conv(u, w, bias):
    kw = w.astype(u.dtype)[:, None, :]
    out = lax.conv_general_dilated(u, kw, window_strides=(1,), padding=[(SSM_CONV - 1, 0)],
                                   dimension_numbers=('NWC', 'WIO', 'NWC'),
                                   feature_group_count=u.shape[-1])
    return out + bias.astype(u.dtype)

def ssd_chunked(x, dt, a, bmat, cmat):
    b, s, h, p = x.shape
    g, nst = bmat.shape[2], bmat.shape[3]
    hg = h // g
    L = SSM_CHUNK
    nc = s // L
    xs = (x.astype(jnp.float32) * dt[..., None]).reshape(b, nc, L, g, hg, p)
    acs = jnp.cumsum((dt * a.astype(jnp.float32)).reshape(b, nc, L, g, hg), axis=2)
    bm = bmat.astype(jnp.float32).reshape(b, nc, L, g, nst)
    cm = cmat.astype(jnp.float32).reshape(b, nc, L, g, nst)
    diff = acs[:, :, :, None] - acs[:, :, None, :]
    causal = jnp.tril(jnp.ones((L, L), dtype=bool))
    decay = jnp.exp(jnp.where(causal[:, :, None, None], diff, NEG_INF))
    cb = jnp.einsum('bclgn,bcsgn->bclsg', cm, bm)
    y_diag = jnp.einsum('bclsg,bclsgh,bcsghp->bclghp', cb, decay, xs)
    decay_st = jnp.exp(acs[:, :, -1:] - acs)
    states = jnp.einsum('bclgn,bclgh,bclghp->bcghpn', bm, decay_st, xs)
    chunk_decay = jnp.exp(acs[:, :, -1])

    def step(carry, inp):
        st, dec = inp
        return carry * dec[..., None, None] + st, carry

    init = jnp.zeros((b, g, hg, p, nst), jnp.float32)
    _, prev = lax.scan(step, init, (states.swapaxes(0, 1), chunk_decay.swapaxes(0, 1)))
    prev = prev.swapaxes(0, 1)
    y_off = jnp.einsum('bclgn,bcghpn,bclgh->bclghp', cm, prev, jnp.exp(acs))
    return (y_diag + y_off).reshape(b, s, h, p)

def hybrid_mixer(h, w_in, b_forget, sinks, conv_w, conv_b, dt_bias, a_log, d_skip,
                 ssm_norm_w, w_out, cos, sin):
    b, s, _ = h.shape
    proj = h @ w_in.astype(h.dtype)
    (q_a, k_a, v_a, g_a, q_b, k_b, v_b, f_b, g_b, z_c, xbc_c, dt_c) = jnp.split(
        proj, _offsets(IN_SPLITS), axis=-1)
    qa = apply_rope(q_a.reshape(b, s, SWA_HEADS, HEAD_DIM), cos, sin)
    ka = apply_rope(k_a.reshape(b, s, SWA_KV_HEADS, HEAD_DIM), cos, sin)
    va = v_a.reshape(b, s, SWA_KV_HEADS, HEAD_DIM)
    ya = sliding_window_attention(qa, ka, va, sinks).reshape(b, s, SWA_W)
    ya = ya * jax.nn.silu(g_a)
    log_f = jax.nn.log_sigmoid(f_b.astype(jnp.float32) + b_forget.astype(jnp.float32))
    yb = forgetting_attention(q_b.reshape(b, s, FOX_HEADS, HEAD_DIM),
                              k_b.reshape(b, s, FOX_HEADS, HEAD_DIM),
                              v_b.reshape(b, s, FOX_HEADS, HEAD_DIM), log_f).reshape(b, s, FOX_W)
    yb = yb * jax.nn.silu(g_b)
    xbc = jax.nn.silu(causal_depthwise_conv(xbc_c, conv_w, conv_b))
    xs, bm, cm = jnp.split(xbc, [SSM_W, SSM_W + SSM_BC_W], axis=-1)
    xs = xs.reshape(b, s, SSM_HEADS, SSM_HEAD_DIM)
    bm = bm.reshape(b, s, SSM_GROUPS, SSM_STATE)
    cm = cm.reshape(b, s, SSM_GROUPS, SSM_STATE)
    dt = jax.nn.softplus(dt_c.astype(jnp.float32) + dt_bias.astype(jnp.float32))
    a = -jnp.exp(a_log.astype(jnp.float32))
    yc = ssd_chunked(xs, dt, a, bm, cm) + d_skip.astype(jnp.float32)[:, None] * xs.astype(jnp.float32)
    yc = yc.reshape(b, s, SSM_W).astype(h.dtype)
    yc = rms_norm(yc * jax.nn.silu(z_c), ssm_norm_w)
    y = jnp.concatenate([ya, yb, yc], axis=-1)
    return y @ w_out.astype(h.dtype)

def memory_cross_attention(h, mem_n, wq, wk, wv, wo):
    b, s, _ = h.shape
    m = mem_n.shape[1]
    q = (h @ wq.astype(h.dtype)).reshape(b, s, MEM_HEADS, MEM_HEAD_DIM)
    k = (mem_n @ wk.astype(h.dtype)).reshape(b, m, MEM_HEADS, MEM_HEAD_DIM)
    v = (mem_n @ wv.astype(h.dtype)).reshape(b, m, MEM_HEADS, MEM_HEAD_DIM)
    logits = jnp.einsum('bqhd,bkhd->bhqk', q, k).astype(jnp.float32) * (MEM_HEAD_DIM ** -0.5)
    probs = jax.nn.softmax(logits, axis=-1).astype(v.dtype)
    out = jnp.einsum('bhqk,bkhd->bqhd', probs, v).reshape(b, s, D_MODEL)
    return out @ wo.astype(h.dtype)

def first_inputs(seed: int = 0) -> dict:
    key = jax.random.key(seed)
    ks = jax.random.split(key, 20)
    f32 = jnp.float32

    def nrm(k, shape, scale):
        return jax.random.normal(k, shape, f32) * scale

    dt0 = jnp.exp(jax.random.uniform(ks[7], (DEPTH, SSM_HEADS), f32, np.log(1e-3), np.log(1e-1)))
    return {
        "x": nrm(ks[0], (BATCH, SEQ, D_MODEL), 1.0),
        "mem": nrm(ks[1], (BATCH, MEM_TOKENS, D_MODEL), 1.0),
        "norm_mix_w": 1.0 + nrm(ks[2], (DEPTH, D_MODEL), 0.02),
        "w_in": nrm(ks[3], (DEPTH, D_MODEL, IN_W), D_MODEL ** -0.5),
        "b_forget": jax.random.uniform(ks[4], (DEPTH, FOX_HEADS), f32, 1.0, 6.0),
        "swa_sinks": nrm(ks[5], (DEPTH, SWA_HEADS), 0.5),
        "conv_w": nrm(ks[6], (DEPTH, SSM_CONV, SSM_CONV_W), SSM_CONV ** -0.5),
        "conv_b": nrm(ks[8], (DEPTH, SSM_CONV_W), 0.02),
        "dt_bias": dt0 + jnp.log(-jnp.expm1(-dt0)),
        "a_log": jnp.log(jax.random.uniform(ks[9], (DEPTH, SSM_HEADS), f32, 1.0, 16.0)),
        "d_skip": 1.0 + nrm(ks[10], (DEPTH, SSM_HEADS), 0.1),
        "ssm_norm_w": 1.0 + nrm(ks[11], (DEPTH, SSM_W), 0.02),
        "w_out": nrm(ks[12], (DEPTH, MIX_WIDTH, D_MODEL), MIX_WIDTH ** -0.5),
        "norm_xq_w": 1.0 + nrm(ks[13], (DEPTH, D_MODEL), 0.02),
        "norm_mem_w": 1.0 + nrm(ks[14], (DEPTH, D_MODEL), 0.02),
        "w_mq": nrm(ks[15], (DEPTH, D_MODEL, D_MODEL), D_MODEL ** -0.5),
        "w_mk": nrm(ks[16], (DEPTH, D_MODEL, D_MODEL), D_MODEL ** -0.5),
        "w_mv": nrm(ks[17], (DEPTH, D_MODEL, D_MODEL), D_MODEL ** -0.5),
        "w_mo": nrm(ks[18], (DEPTH, D_MODEL, D_MODEL), D_MODEL ** -0.5),
        "final_norm_w": 1.0 + nrm(ks[19], (D_MODEL,), 0.02),
    }

def first_block(x, mem, norm_mix_w, w_in, b_forget, swa_sinks, conv_w, conv_b, dt_bias, a_log,
              d_skip, ssm_norm_w, w_out, norm_xq_w, norm_mem_w, w_mq, w_mk, w_mv, w_mo,
              final_norm_w):
    cos, sin = rope_tables(x.shape[1])
    for l in range(DEPTH):
        h = rms_norm(x, norm_mix_w[l])
        x = x + hybrid_mixer(h, w_in[l], b_forget[l], swa_sinks[l], conv_w[l], conv_b[l],
                             dt_bias[l], a_log[l], d_skip[l], ssm_norm_w[l], w_out[l], cos, sin)
        hq = rms_norm(x, norm_xq_w[l])
        mem_n = rms_norm(mem, norm_mem_w[l])
        x = x + memory_cross_attention(hq, mem_n, w_mq[l], w_mk[l], w_mv[l], w_mo[l])
    return rms_norm(x, final_norm_w)


GRID_W = 64
CTX_LEN = 256
NA_HEADS = 6
NA_DIM = NA_HEADS * HEAD_DIM
NA_ROWS = 8
NA_COLS = 16
NA_QBLOCK = 16
NA_KSPAN = 32
HG_HEADS = 6
HG_DK = 64
HG_DV = 64
HG_DIM = HG_HEADS * HG_DV
HG_CHUNK = 64
CONV_DIM = 256
CONV_WIDTH = 3
MIX_DIM = NA_DIM + HG_DIM + CONV_DIM
N_EXPERTS = 16
EXPERT_DIM = 512
EC_CAPACITY_FACTOR = 2
ROPE_BASE = 10000.0
NORM_EPS = 1e-6
N_MOD = 6


def _in_sizes():
    return [NA_DIM] * 3 + [HG_HEADS * HG_DK] * 3 + [HG_HEADS * HG_DV] * 2 + [CONV_DIM] * 3

def _split_points():
    return [int(s) for s in np.cumsum(_in_sizes())[:-1]]

def _rmsnorm(x, w):
    xf = x.astype(jnp.float32)
    y = xf * lax.rsqrt(jnp.mean(xf * xf, axis=-1, keepdims=True) + NORM_EPS)
    return (y * w.astype(jnp.float32)).astype(x.dtype)

def _adaln(cond, w, b):
    return jnp.matmul(jax.nn.silu(cond), w) + b

def _modulate(h, shift, scale):
    return h * (1 + scale) + shift

def _rope_tables(n, dtype):
    t = jnp.arange(n, dtype=jnp.int32)
    row = (t // GRID_W).astype(jnp.float32)
    col = (t % GRID_W).astype(jnp.float32)
    n_freq = HEAD_DIM // 4
    inv = ROPE_BASE ** (-jnp.arange(n_freq, dtype=jnp.float32) / n_freq)
    ar = row[:, None] * inv
    ac = col[:, None] * inv
    ang = jnp.concatenate([ar, ar, ac, ac], axis=-1)
    return jnp.cos(ang).astype(dtype)[:, None, :], jnp.sin(ang).astype(dtype)[:, None, :]

def _rot(x):
    x0, x1, x2, x3 = jnp.split(x, 4, axis=-1)
    return jnp.concatenate([-x1, x0, -x3, x2], axis=-1)

def _rope(x, cos, sin):
    return x * cos + _rot(x) * sin

def _na_col_tables():
    cols = np.arange(GRID_W)
    win_start = np.clip(cols - NA_COLS // 2, 0, GRID_W - NA_COLS)
    n_cb = GRID_W // NA_QBLOCK
    blk_start = np.clip(win_start[::NA_QBLOCK], 0, GRID_W - NA_KSPAN)
    key_cols = blk_start[:, None] + np.arange(NA_KSPAN)[None, :]
    q_cols = cols.reshape(n_cb, NA_QBLOCK)
    q_start = win_start.reshape(n_cb, NA_QBLOCK)
    kc = key_cols[:, None, :]
    mask = (kc >= q_start[..., None]) & (kc < q_start[..., None] + NA_COLS)
    rel = np.clip(kc - q_cols[..., None] + NA_COLS - 1, 0, 2 * NA_COLS - 2)
    return key_cols, rel, mask

def _na_latent(q, k, v, k_ctx, v_ctx, rpb):
    b, n, h, d = q.shape
    rows = n // GRID_W
    kr = min(NA_ROWS, rows)
    n_cb = GRID_W // NA_QBLOCK
    key_cols_np, rel_col_np, col_mask_np = _na_col_tables()
    key_cols = jnp.asarray(key_cols_np)
    rel_col = jnp.asarray(rel_col_np)
    n_loc = kr * NA_KSPAN
    win_mask = jnp.asarray(np.broadcast_to(col_mask_np[:, :, None, :], (n_cb, NA_QBLOCK, kr, NA_KSPAN)).reshape(n_cb, NA_QBLOCK, n_loc))
    kg = k.reshape(b, rows, GRID_W, h, d)
    vg = v.reshape(b, rows, GRID_W, h, d)
    q_rows = q.reshape(b, rows, n_cb, NA_QBLOCK, h, d).transpose(1, 0, 2, 3, 4, 5)
    scale = d ** -0.5

    def gather_blocks(g, rs):
        blk = lax.dynamic_slice_in_dim(g, rs, kr, axis=1)[:, :, key_cols]
        return blk.transpose(0, 2, 1, 3, 4, 5).reshape(b, n_cb, n_loc, h, d)

    def row_fn(xs):
        r, q_r = xs
        rs = jnp.clip(r - kr // 2, 0, rows - kr)
        k_loc = gather_blocks(kg, rs)
        v_loc = gather_blocks(vg, rs)
        rel_row = rs + jnp.arange(kr) - r + (NA_ROWS - 1)
        bias = rpb[:, rel_row[:, None, None, None], rel_col[None]]
        bias = bias.transpose(0, 2, 3, 1, 4).reshape(h, n_cb, NA_QBLOCK, n_loc)
        s_loc = jnp.einsum('bjqhd,bjkhd->bhjqk', q_r, k_loc).astype(jnp.float32) * scale + bias.astype(jnp.float32)
        s_loc = jnp.where(win_mask, s_loc, -jnp.inf)
        s_ctx = jnp.einsum('bjqhd,bchd->bhjqc', q_r, k_ctx).astype(jnp.float32) * scale
        p = jax.nn.softmax(jnp.concatenate([s_loc, s_ctx], axis=-1), axis=-1).astype(v.dtype)
        o_loc = jnp.einsum('bhjqk,bjkhd->bjqhd', p[..., :n_loc], v_loc)
        o_ctx = jnp.einsum('bhjqc,bchd->bjqhd', p[..., n_loc:], v_ctx)
        return o_loc + o_ctx

    out = lax.map(row_fn, (jnp.arange(rows, dtype=jnp.int32), q_rows))
    return out.transpose(1, 0, 2, 3, 4, 5).reshape(b, n, h, d)

def _ctx_attn(q, k, v):
    s = jnp.einsum('bqhd,bkhd->bhqk', q, k).astype(jnp.float32) * (q.shape[-1] ** -0.5)
    p = jax.nn.softmax(s, axis=-1).astype(v.dtype)
    return jnp.einsum('bhqk,bkhd->bqhd', p, v)

def _hgrn_lower_bounds(logits):
    p = jax.nn.softmax(logits.astype(jnp.float32), axis=1)
    return jnp.concatenate([jnp.zeros_like(p[:, :1]), jnp.cumsum(p[:, 1:], axis=1)], axis=1)

def _hgrn_gates(f_logit, lb):
    z = f_logit.astype(jnp.float32)
    log_f = jnp.logaddexp(jnp.log(lb), jnp.log1p(-lb) + jax.nn.log_sigmoid(z))
    k = (1 - lb) * jax.nn.sigmoid(-z)
    return log_f, k

def _heads(a, dh):
    return a.reshape(a.shape[0], a.shape[1], -1, dh).astype(jnp.float32)

def _gla_scan(q, k, log_f, v, s0):
    b, t, h, _ = q.shape
    nc = t // HG_CHUNK

    def to_chunks(a):
        return a.reshape(b, nc, HG_CHUNK, h, a.shape[-1]).transpose(1, 0, 3, 2, 4)

    causal = jnp.tril(jnp.ones((HG_CHUNK, HG_CHUNK), dtype=bool))

    def step(s, xs):
        qc, kc, gc, vc = xs
        a = jnp.cumsum(gc, axis=2)
        diff = a[:, :, :, None, :] - a[:, :, None, :, :]
        decay = jnp.exp(jnp.where(causal[:, :, None], diff, -jnp.inf))
        scores = jnp.sum(qc[:, :, :, None, :] * kc[:, :, None, :, :] * decay, axis=-1)
        o = jnp.einsum('bhts,bhsv->bhtv', scores, vc) + jnp.einsum('bhtk,bhkv->bhtv', qc * jnp.exp(a), s)
        a_last = a[:, :, -1:, :]
        s_new = jnp.exp(a_last[:, :, 0, :, None]) * s + jnp.einsum('bhsk,bhsv->bhkv', kc * jnp.exp(a_last - a), vc)
        return s_new, o

    s_fin, o = lax.scan(step, s0, (to_chunks(q), to_chunks(k), to_chunks(log_f), to_chunks(v)))
    o = o.transpose(1, 0, 3, 2, 4).reshape(b, t, h, v.shape[-1])
    return o, s_fin

def _hgrn2_mixer(lat, cxt, lb_fwd, lb_bwd, norm_w, need_ctx):
    q_l, ff_l, fb_l, i_l, g_l = lat
    q_c, ff_c, fb_c, i_c, g_c = cxt
    dtype = q_l.dtype
    b = q_l.shape[0]
    scale = HG_DK ** -0.5
    ql = _heads(q_l, HG_DK) * scale
    qc = _heads(q_c, HG_DK) * scale
    vl = _heads(i_l, HG_DV)
    vc = _heads(i_c, HG_DV)
    o_l = jnp.zeros_like(vl)
    o_c = jnp.zeros_like(vc)
    for f_lat, f_ctx, lb, rev in ((ff_l, ff_c, lb_fwd, False), (fb_l, fb_c, lb_bwd, True)):
        lb = lb.astype(jnp.float32).reshape(HG_HEADS, HG_DK)
        lf_l, k_l = _hgrn_gates(_heads(f_lat, HG_DK), lb)
        lf_c, k_c = _hgrn_gates(_heads(f_ctx, HG_DK), lb)
        lat_seq = (ql, k_l, lf_l, vl)
        ctx_seq = (qc, k_c, lf_c, vc)
        if rev:
            lat_seq = tuple(jnp.flip(a, axis=1) for a in lat_seq)
            ctx_seq = tuple(jnp.flip(a, axis=1) for a in ctx_seq)
        s0 = jnp.zeros((b, HG_HEADS, HG_DK, HG_DV), jnp.float32)
        oc, s_ctx = _gla_scan(*ctx_seq, s0)
        ol, _ = _gla_scan(*lat_seq, s_ctx)
        if rev:
            oc = jnp.flip(oc, axis=1)
            ol = jnp.flip(ol, axis=1)
        o_l = o_l + ol
        o_c = o_c + oc
    y_l = (_rmsnorm(o_l, norm_w) * jax.nn.silu(_heads(g_l, HG_DV))).reshape(g_l.shape).astype(dtype)
    if not need_ctx:
        return y_l, None
    y_c = (_rmsnorm(o_c, norm_w) * jax.nn.silu(_heads(g_c, HG_DV))).reshape(g_c.shape).astype(dtype)
    return y_l, y_c

def _short_gated_conv(b_gate, c_gate, u, w):
    z = c_gate * u
    t = z.shape[1]
    zp = jnp.pad(z, ((0, 0), (CONV_WIDTH // 2, CONV_WIDTH // 2), (0, 0)))
    y = sum(w[j] * zp[:, j:j + t] for j in range(CONV_WIDTH))
    return b_gate * y

def _token_mixers(h, hc, w_in_l, q_norm, k_norm, rpb, lb_fwd, lb_bwd, hg_norm_l, conv_w_l, rope_cos, rope_sin, need_ctx):
    b, n, _ = h.shape
    ctx_len = hc.shape[1]
    pts = _split_points()
    p = jnp.split(jnp.einsum('btd,dk->btk', h, w_in_l), pts, axis=-1)
    pc = jnp.split(jnp.einsum('btd,dk->btk', hc, w_in_l), pts, axis=-1)

    def na_heads(a):
        return a.reshape(a.shape[0], a.shape[1], NA_HEADS, HEAD_DIM)

    q = _rope(_rmsnorm(na_heads(p[0]), q_norm), rope_cos, rope_sin)
    k = _rope(_rmsnorm(na_heads(p[1]), k_norm), rope_cos, rope_sin)
    v = na_heads(p[2])
    qc = _rmsnorm(na_heads(pc[0]), q_norm)
    kc = _rmsnorm(na_heads(pc[1]), k_norm)
    vc = na_heads(pc[2])
    na = _na_latent(q, k, v, kc, vc, rpb).reshape(b, n, NA_DIM)
    hg, hg_c = _hgrn2_mixer(p[3:8], pc[3:8], lb_fwd, lb_bwd, hg_norm_l, need_ctx)
    cv = _short_gated_conv(p[8], p[9], p[10], conv_w_l)
    mix = jnp.concatenate([na, hg, cv], axis=-1)
    if not need_ctx:
        return mix, None
    na_c = _ctx_attn(qc, kc, vc).reshape(b, ctx_len, NA_DIM)
    cv_c = _short_gated_conv(pc[8], pc[9], pc[10], conv_w_l)
    return mix, jnp.concatenate([na_c, hg_c, cv_c], axis=-1)

def _expert_choice_ffn(h, w_router, w_gate, w_up, w_down):
    b, t, d = h.shape
    cap = EC_CAPACITY_FACTOR * t // N_EXPERTS
    aff = jax.nn.softmax(jnp.einsum('btd,de->bte', h, w_router).astype(jnp.float32), axis=-1)
    vals, idx = lax.top_k(aff.transpose(0, 2, 1), cap)
    xg = jax.vmap(lambda hb, ib: hb[ib])(h, idx)
    hid = jax.nn.silu(jnp.einsum('becd,edf->becf', xg, w_gate)) * jnp.einsum('becd,edf->becf', xg, w_up)
    out = jnp.einsum('becf,efd->becd', hid, w_down) * vals[..., None].astype(h.dtype)
    return jax.vmap(lambda ob, ib: jnp.zeros((t, d), h.dtype).at[ib.reshape(-1)].add(ob.reshape(-1, d)))(out, idx)

def second_inputs(seed: int = 0) -> dict:
    key = jax.random.key(seed)
    ks = jax.random.split(key, 20)
    nrm = jax.random.normal
    d = D_MODEL
    in_cols = sum(_in_sizes())
    return {
        'x': nrm(ks[0], (BATCH, SEQ, d), jnp.float32),
        'c': nrm(ks[1], (BATCH, d), jnp.float32),
        'ctx': nrm(ks[2], (BATCH, CTX_LEN, d), jnp.float32),
        'c_ctx': nrm(ks[3], (d,), jnp.float32),
        'w_mod': nrm(ks[4], (DEPTH, d, N_MOD * d), jnp.float32) * (0.5 * d ** -0.5),
        'b_mod': 0.02 * nrm(ks[5], (DEPTH, N_MOD * d), jnp.float32),
        'norm1_w': 1.0 + 0.1 * nrm(ks[6], (DEPTH, d), jnp.float32),
        'w_in': nrm(ks[7], (DEPTH, d, in_cols), jnp.float32) * d ** -0.5,
        'na_q_norm': 1.0 + 0.1 * nrm(ks[8], (DEPTH, HEAD_DIM), jnp.float32),
        'na_k_norm': 1.0 + 0.1 * nrm(ks[9], (DEPTH, HEAD_DIM), jnp.float32),
        'na_rpb': 0.5 * nrm(ks[10], (DEPTH, NA_HEADS, 2 * NA_ROWS - 1, 2 * NA_COLS - 1), jnp.float32),
        'hg_lb_logits': nrm(ks[11], (2, DEPTH, HG_HEADS * HG_DK), jnp.float32),
        'hg_norm': 1.0 + 0.1 * nrm(ks[12], (DEPTH, HG_DV), jnp.float32),
        'conv_w': nrm(ks[13], (DEPTH, CONV_WIDTH, CONV_DIM), jnp.float32) * CONV_WIDTH ** -0.5,
        'w_out': nrm(ks[14], (DEPTH, MIX_DIM, d), jnp.float32) * MIX_DIM ** -0.5,
        'norm2_w': 1.0 + 0.1 * nrm(ks[15], (DEPTH, d), jnp.float32),
        'w_router': nrm(ks[16], (DEPTH, d, N_EXPERTS), jnp.float32) * d ** -0.5,
        'w_exp_gate': nrm(ks[17], (DEPTH, N_EXPERTS, d, EXPERT_DIM), jnp.float32) * d ** -0.5,
        'w_exp_up': nrm(ks[18], (DEPTH, N_EXPERTS, d, EXPERT_DIM), jnp.float32) * d ** -0.5,
        'w_exp_down': nrm(ks[19], (DEPTH, N_EXPERTS, EXPERT_DIM, d), jnp.float32) * EXPERT_DIM ** -0.5,
    }

def second_block(x, c, ctx, c_ctx, w_mod, b_mod, norm1_w, w_in, na_q_norm, na_k_norm, na_rpb, hg_lb_logits, hg_norm, conv_w, w_out, norm2_w, w_router, w_exp_gate, w_exp_up, w_exp_down):
    n = x.shape[1]
    rope_cos, rope_sin = _rope_tables(n, x.dtype)
    lb = _hgrn_lower_bounds(hg_lb_logits)
    cx = ctx
    for l in range(DEPTH):
        need_ctx = l < DEPTH - 1
        m_lat = jnp.split(_adaln(c, w_mod[l], b_mod[l])[:, None, :], N_MOD, axis=-1)
        m_ctx = jnp.split(_adaln(c_ctx, w_mod[l], b_mod[l]), N_MOD, axis=-1)
        h = _modulate(_rmsnorm(x, norm1_w[l]), m_lat[0], m_lat[1])
        hc = _modulate(_rmsnorm(cx, norm1_w[l]), m_ctx[0], m_ctx[1])
        mix, mix_c = _token_mixers(h, hc, w_in[l], na_q_norm[l], na_k_norm[l], na_rpb[l], lb[0, l], lb[1, l], hg_norm[l], conv_w[l], rope_cos, rope_sin, need_ctx)
        x = x + m_lat[2] * jnp.einsum('btm,md->btd', mix, w_out[l])
        h2 = _modulate(_rmsnorm(x, norm2_w[l]), m_lat[3], m_lat[4])
        x = x + m_lat[5] * _expert_choice_ffn(h2, w_router[l], w_exp_gate[l], w_exp_up[l], w_exp_down[l])
        if need_ctx:
            cx = cx + m_ctx[2] * jnp.einsum('btm,md->btd', mix_c, w_out[l])
            hc2 = _modulate(_rmsnorm(cx, norm2_w[l]), m_ctx[3], m_ctx[4])
            cx = cx + m_ctx[5] * _expert_choice_ffn(hc2, w_router[l], w_exp_gate[l], w_exp_up[l], w_exp_down[l])
    return x


def setup_inputs(seed=0):
    out = dict(first_inputs(seed))
    for name, value in second_inputs(seed + 1).items():
        if name != "x":
            out[name + "_2"] = value
    return out


def reference(
    x, mem, norm_mix_w, w_in, b_forget, swa_sinks, conv_w, conv_b, dt_bias, a_log, d_skip,
    ssm_norm_w, w_out, norm_xq_w, norm_mem_w, w_mq, w_mk, w_mv, w_mo, final_norm_w, c_2, ctx_2,
    c_ctx_2, w_mod_2, b_mod_2, norm1_w_2, w_in_2, na_q_norm_2, na_k_norm_2, na_rpb_2,
    hg_lb_logits_2, hg_norm_2, conv_w_2, w_out_2, norm2_w_2, w_router_2, w_exp_gate_2,
    w_exp_up_2, w_exp_down_2,
):
    x = first_block(
        x, mem, norm_mix_w, w_in, b_forget, swa_sinks, conv_w, conv_b, dt_bias, a_log, d_skip,
        ssm_norm_w, w_out, norm_xq_w, norm_mem_w, w_mq, w_mk, w_mv, w_mo, final_norm_w,
    )
    return second_block(
        x, c_2, ctx_2, c_ctx_2, w_mod_2, b_mod_2, norm1_w_2, w_in_2, na_q_norm_2, na_k_norm_2,
        na_rpb_2, hg_lb_logits_2, hg_norm_2, conv_w_2, w_out_2, norm2_w_2, w_router_2,
        w_exp_gate_2, w_exp_up_2, w_exp_down_2,
    )


_drawn_inputs = setup_inputs


def setup_inputs(seed=0):
    import zlib

    import numpy as np

    out = dict(_drawn_inputs(seed))
    spreads = {}
    factors = {'swa_sinks': 8.0,
     'ssm_norm_w': 2.934,
     'norm_xq_w': 8.0,
     'norm_mem_w': 8.0,
     'ctx_2': 2.879,
     'na_q_norm_2': 8.0,
     'na_k_norm_2': 8.0,
     'na_rpb_2': 6.704,
     'hg_norm_2': 2.961}
    for name, (base, spread) in spreads.items():
        noise = np.random.default_rng([zlib.crc32(name.encode()), seed]).standard_normal(out[name].shape)
        drawn = base * np.exp(spread * noise) if base else spread * noise
        out[name] = jnp.asarray(drawn.astype(out[name].dtype))
    for name, factor in factors.items():
        out[name] = (out[name] * factor).astype(out[name].dtype)
    return out
```

```python
import concourse.bass as bass
from concourse import mybir
from contextlib import ExitStack
import numpy as np

P = 128
D_MODEL, SEQ, DEPTH, MEM, CTX = 1024, 512, 2, 256, 256
KT = D_MODEL // P
ALL = SEQ + CTX
HD = 64
EPS = 1e-6
NEG = -1e30
GRID, NA_COLS, RPB_ROWS = 64, 16, 15
NA_HEADS, HG_PAIRS, N_EXPERTS, EXPERT_DIM = 6, 3, 16, 512
CAP, CAP_CTX = 2 * SEQ // N_EXPERTS, 2 * CTX // N_EXPERTS
SLOTS = CAP + CAP_CTX
LEVELS = (64, 32, 16, 8, 4, 2, 1)

C_IDENT, C_ONES, C_HEADS, C_ROT1, C_ROT2 = 0, 128, 256, 384, 512
C_CAUSAL, C_PREV, C_LOWER = 640, 768, 896
C_LEVEL, C_LEVEL_BACK, C_COLMASK = 1024, 2048, 3072
C_SLOT, C_SLOTROW, C_TAB = 3136, 3138, 3202
N_CONST = C_TAB + 2 * ALL

(A_MIX, A_XQ, A_MEM, A_SSM, A_CONV, A_CONVB, A_SKIP, A_SINK, A_GATE, A_ALOG, A_FINAL) = (
    0, 8, 16, 24, 32, 80, 92, 100, 108, 109, 110)
N_PAR1 = 118
(B_MOD, B_N1, B_N2, B_QN, B_KN, B_HGN, B_LB, B_CONV) = (0, 48, 56, 64, 65, 66, 67, 79)
B_COND = 85
N_PAR2 = B_COND + 16

RING = 8
EXPERT_UNITS = 12
RPB_AT, RPB_WIDTH = 6912, NA_HEADS * 14 * GRID


def build(nc, names, out):
    f32 = mybir.dt.float32
    ALU, ACT, AX = mybir.AluOpType, mybir.ActivationFunctionType, mybir.AxisListType
    T = SEQ
    ctx = ExitStack()
    with ctx:
        def sb(name, width):
            return ctx.enter_context(nc.sbuf_tensor(name, [P, width], f32))

        x_sb = sb("x_sb", KT * ALL)
        h_sb = sb("h_sb", KT * ALL)
        x = x_sb[:, :].rearrange("p (k t) -> p k t", k=KT)
        h = h_sb[:, :].rearrange("p (k t) -> p k t", k=KT)
        y_sb = sb("y_sb", 16 * T)
        y = y_sb[:, :].rearrange("p (k t) -> p k t", k=16)
        work = sb("work", 12800)
        ring = sb("ring", RING * 1024)
        const = sb("const", N_CONST)
        par = sb("par", DEPTH * (N_PAR1 + N_PAR2))
        prob = sb("prob", 2 * ALL)
        probT = sb("probT", 2 * ALL)
        cpad = sb("cpad", 2 * (T + 4))
        small = sb("small", 512)
        rstd = sb("rstd", ALL)
        acc_o = sb("acc_o", ALL)
        banks = [ctx.enter_context(nc.psum_tensor(f"bank{i}", [P, 512], f32)) for i in range(8)]

        def cst(at, n=P, rows=P):
            return const[0:rows, at:at + n]

        ident = cst(C_IDENT)

        def flat(at, n):
            return work[:, at:at + n]

        def tiles(at, k, n):
            return work[:, at:at + k * n].rearrange("p (k t) -> p k t", k=k)

        def sem(name):
            return ctx.enter_context(nc.semaphore(name))

        w_loaded = [sem(f"w_loaded{i}") for i in range(RING)]
        w_turn = sem("w_turn")
        inputs_in = sem("inputs_in")
        out_done = sem("out_done")
        ctx_in = sem("ctx_in")
        table_in = sem("table_in")
        table_room = sem("table_room")
        act_output2 = sem("act_output2")
        one_hot_ready = sem("one_hot_ready")
        scaled_ready = sem("scaled_ready")
        state_ready = sem("state_ready")
        scores_ready = sem("scores_ready")
        result_ready = sem("result_ready")
        full_for_act, full_for_dve = sem("full_for_act"), sem("full_for_dve")
        freed_by_act, freed_by_dve = sem("freed_by_act"), sem("freed_by_dve")
        act_step, dve_step = sem("act_step"), sem("dve_step")
        squares_ready = sem("squares_ready")
        variance_ready = sem("variance_ready")
        root_ready = sem("root_ready")
        operand_ready = sem("operand_ready")
        max_ready = sem("max_ready")
        exp_ready = sem("exp_ready")
        prob_ready = sem("prob_ready")
        act_input = sem("act_input")
        act_output = sem("act_output")
        raw_ready = sem("raw_ready")
        head_done = sem("head_done")
        memory_read = sem("memory_read")

        UNITS = {"swa": 10, "fox": 17, "ssm": 20, "out1": 16, "mem": 32,
                 "mod": 48, "conv": 6, "na": 9, "hgrn": 15, "out2": 8, "moe": 1 + N_EXPERTS * EXPERT_UNITS}
        PHASES = list(UNITS)
        stack = ExitStack()
        block = stack.enter_context(nc.Block())

        class Engine:

            def __init__(self, eng, step):
                self.eng, self.step, self.done, self.awaited = eng, step, {}, {}

            def nth(self, s):
                self.awaited[s.name] = self.awaited.get(s.name, 0) + 1
                return self.awaited[s.name]

            def notify(self, s):
                self.done[s.name] = self.done.get(s.name, 0) + 1
                self.eng.sem_inc(s, 1)

            def link(self, ins, s=None, wait=True):
                s = s or self.step
                self.done[s.name] = self.done.get(s.name, 0) + 1
                ins.then_inc(s, 1)
                if wait:
                    self.eng.wait_ge(s, self.done[s.name])

        def swa_units(l):
            q, k, v = tiles(0, 4, T), tiles(2048, 1, T), tiles(2560, 4, P)
            for t in range(4):
                for half in range(2):
                    r = slice(64 * half, 64 * half + 64)
                    for i in range(T // P):
                        blocks = [i] if i == 0 else [i - 1, i]
                        at = []
                        for n, b in enumerate(blocks):
                            at.append((0, n * P, P, [
                                (q[r, t, i * P:(i + 1) * P], k[r, 0, b * P:(b + 1) * P]),
                                (ident, cst(C_CAUSAL) if b == i else cst(C_PREV))]))
                        yield dict(parts=at, nk=len(blocks) * P, sink=4 * half + t,
                                   v=[v[:, b, r] for b in blocks],
                                   outs=[(t, r, i)], closes=half == 1 and i == 3, gate=t, l=l)

        def fox_units():
            q, k, v = tiles(3072, 4, T), tiles(5120, 4, T), tiles(7168, 4, T)
            c, negc = flat(9216, T), flat(9728, T)
            for t in range(4):
                for half in range(2):
                    r = slice(64 * half, 64 * half + 64)
                    hh = 2 * t + half
                    one = const[0:8, C_IDENT + hh:C_IDENT + hh + 1]
                    for i in range(T // P):
                        n = (i + 1) * P
                        qi = slice(i * P, n)
                        at = [(0, 0, n, [(q[r, t, qi], k[r, t, 0:n]),
                                         (one.to_broadcast([8, P]), negc[0:8, 0:n]),
                                         (c[0:8, qi], one.to_broadcast([8, n]))], (ident, cst(C_CAUSAL), i * P))]
                        yield dict(parts=at, nk=n, sink=None,
                                   v=[v[:, b, hh * 64:hh * 64 + 64] for b in range(i + 1)],
                                   outs=[(t, r, i)], closes=half == 1 and i == 3, gate=4 + t)

        def mem_units():
            q, k, v = tiles(0, 8, T), tiles(4096, 8, MEM), tiles(6144, 2, D_MODEL)
            for hh in range(4):
                for i in range(T // P):
                    at = [(0, 0, MEM, [(q[:, 2 * hh + j, i * P:(i + 1) * P], k[:, 2 * hh + j, :]) for j in range(2)])]
                    yield dict(parts=at, nk=MEM, sink=None,
                               v=[v[:, b, hh * 256:hh * 256 + 256] for b in range(2)],
                               outs=[(2 * hh + j, slice(0, P), i) for j in range(2)],
                               closes=i == 3, gate=None, dest=[2 * hh, 2 * hh + 1])

        @block.sync
        def _(sp):
            sp.dma_start(const[:, :], names["consts"]).then_inc(inputs_in, 16)
            sp.dma_start(x[:, :, 0:T], names["xT"].rearrange("(k p) t -> p k t", p=P)).then_inc(inputs_in, 16)
            sp.dma_start(x[:, :, T:ALL], names["memT"].rearrange("(k p) t -> p k t", p=P)).then_inc(inputs_in, 16)
            sp.dma_start(par[:, :], names["params"]).then_inc(inputs_in, 16)
            unit = 0
            for blk, l, phase in [(1, l, p) for l in range(DEPTH) for p in PHASES[:5]] + [
                    (2, l, p) for l in range(DEPTH) for p in PHASES[5:]]:
                if blk == 2 and l == 0 and phase == "mod":
                    sp.wait_ge(memory_read, DEPTH)
                    sp.dma_start(x[:, :, T:ALL], names["ctxT"].rearrange("(k p) t -> p k t", p=P)).then_inc(ctx_in, 16)
                    sp.dma_start(cst(C_TAB, 2 * ALL), names["tables2"]).then_inc(ctx_in, 16)
                if blk == 2 and phase == "mod":
                    sp.wait_ge(table_room, l + 1)
                    sp.dma_start(work[:, RPB_AT:RPB_AT + RPB_WIDTH], names["bias"][l]).then_inc(table_in, 16)
                for _ in range(UNITS[phase]):
                    if unit >= RING:
                        sp.wait_ge(w_turn, unit - RING + 2)
                    sp.dma_start(ring[:, unit % RING * 1024:(unit % RING + 1) * 1024],
                                 names["stream"][unit]).then_inc(w_loaded[unit % RING], 16)
                    unit += 1
            sp.wait_ge(result_ready, 1)
            sp.dma_start(out.rearrange("(k p) t -> p k t", p=P), x[:, :, 0:T]).then_inc(out_done, 16)
            sp.wait_ge(out_done, 16)

        def par1(l, at, n=1, rows=slice(0, P)):
            return par[rows, l * N_PAR1 + at:l * N_PAR1 + at + n]

        def par2(l, at, n=1, rows=slice(0, P)):
            base = DEPTH * N_PAR1 + l * N_PAR2
            return par[rows, base + at:base + at + n]

        FD, CHUNKS, HEADS = slice(32, 48), SEQ // P, 16
        xbc = tiles(0, 12, T)
        xs_tok, b_tok = tiles(6144, CHUNKS, D_MODEL), tiles(10240, 8, P)
        prev = h_sb[:, 0:3072].rearrange("p (c n) -> p c n", c=3)
        xs_dec = h_sb[:, 3072:4096].rearrange("p (r n) -> p r n", r=2)
        e_off = h_sb[:, 4096:5120].rearrange("p (r n) -> p r n", r=2)
        diff = h_sb[:, 5120:6144].rearrange("p (r n) -> p r n", r=2)
        m_dec = prob[:, 0:1024].rearrange("p (r n) -> p r n", r=2)
        c_off = probT[:, 0:1024].rearrange("p (r n) -> p r n", r=2)
        cbm = cpad[:, 0:1024].rearrange("p (g n) -> p g n", g=2)
        gates = flat(11264, T)
        acs = flat(11776, T)
        gtmp = flat(12288, T)
        tok = small[:, 0:192]
        w_st, chunk_decay = small[:, 192:256], small[:, 256:320]
        a_neg = small[FD, 320:321]
        nmax, rsum, rinv, sinkp = (small[:, 324 + 4 * i:328 + 4 * i] for i in range(4))
        eps_col = small[:, 340:341]

        modv, mod_a = small[:, 344:440], small[:, 440:472]
        csil = small[:, 472:488]
        mod_rows = work[0:2, 0:6 * D_MODEL]
        lbv = small[:, 488:500]
        moe_small = small[:, 0:320]
        mix = y_sb[:, 0:KT * ALL].rearrange("p (k t) -> p k t", k=KT)
        SPANS = (slice(0, T), slice(T, ALL))
        na_q, na_k, na_v = tiles(0, 3, ALL), tiles(3 * ALL, 3, ALL), tiles(6 * ALL, 6, 384)
        head_sq = y_sb[:, 0:6 * ALL].rearrange("p (k t) -> p k t", k=6)
        bias_table = flat(RPB_AT, RPB_WIDTH)
        hg_q, hg_z, hg_v = tiles(0, 3, ALL), tiles(3 * ALL, 6, ALL), tiles(9 * ALL, 6, 384)
        hg_a = h_sb[:, 0:6 * ALL].rearrange("p (k t) -> p k t", k=6)
        hg_tmp = tiles(12 * ALL, 3, ALL)
        scaled = ([flat(12 * ALL + n * ALL, ALL) for n in range(4)]
                  + [h_sb[:, (6 + n) * ALL:(7 + n) * ALL] for n in range(2)] + [rstd[:, :]])
        q_exp, k_exp, k_tok = y_sb[:, 6144:6912], cpad[:, 0:ALL], y_sb[:, 6912:7680]
        products = [prob[:, 0:1024], probT[:, 0:1024]]
        sums_st = prob[:, 1024:1536]
        state, state_new = y_sb[:, 7680:7808], y_sb[:, 7808:7936]
        last_dec = y_sb[:, 7936:7942]
        last_sum = y_sb[:, 7942:7948]
        N_CH = ALL // P
        FLOW = ([4, 5, 0, 1, 2, 3], [5, 4, 3, 2, 1, 0])

        def need_ctx(l):
            return l < DEPTH - 1

        def wanted(l, chunk):
            return need_ctx(l) or chunk < T // P

        def modc(m, k, s):
            return modv[:, (m * KT + k) * 2 + s:(m * KT + k) * 2 + s + 1]

        def na_units():
            for hh in range(NA_HEADS):
                p, r = hh // 2, slice(hh % 2 * 64, hh % 2 * 64 + 64)
                for t in range(4):
                    qt = na_q[r, p, t * P:(t + 1) * P]
                    table = bias_table.rearrange("p (h a c) -> p h a c", h=NA_HEADS, a=14)[:, hh, 6 - 2 * t:14 - 2 * t, :]
                    yield dict(parts=[(0, 0, T, [(qt, na_k[r, p, 0:T])]), (1, 0, CTX, [(qt, na_k[r, p, T:ALL])])],
                               nk=ALL, sink=None, bias=True, local=table,
                               v=[na_v[:, j, hh * 64:hh * 64 + 64] for j in range(6)],
                               outs=[(p, r, t)], closes=hh % 2 == 1 and t == 3, gate=None, dest=[mix[:, p, 0:T]])

        def ctx_units():
            for hh in range(NA_HEADS):
                p, r = hh // 2, slice(hh % 2 * 64, hh % 2 * 64 + 64)
                for t in range(2):
                    qt = na_q[r, p, T + t * P:T + (t + 1) * P]
                    yield dict(parts=[(1, 0, CTX, [(qt, na_k[r, p, T:ALL])])],
                               nk=CTX, sink=None, bias=True, local=None,
                               v=[na_v[:, 4 + j, hh * 64:hh * 64 + 64] for j in range(2)],
                               outs=[(p, r, t)], closes=hh % 2 == 1 and t == 1, gate=None, dest=[mix[:, p, T:ALL]])

        h_tok = tiles(0, 6, D_MODEL)
        QUAD = 4
        one_hot, one_hot_c = tiles(6144, 4, QUAD * CAP), tiles(7168, 2, QUAD * CAP_CTX)
        silu_g = [flat(7424 + n * 384, 384) for n in range(2)]
        hidden = [flat(8192 + n * 384, 384) for n in range(2)]
        aff_t, left, ranks, vals = (work[0:16, 8960 + n * ALL:8960 + (n + 1) * ALL] for n in range(4))
        gathered = [v.rearrange("p (e k s) -> p e k s", e=2, k=KT) for v in (h_sb[:, 4096:5632], probT[:, :])]
        out_e = y_sb[:, :].rearrange("p (e n) -> p e n", e=8)
        out_c = h_sb[:, 0:4096].rearrange("p (e n) -> p e n", e=4)
        aff = moe_small[:, 0:96]
        rank_tok = moe_small[:, 96:192]
        row_max, row_sum = moe_small[:, 192:198], moe_small[:, 198:204]
        top8 = small[0:16, 208:216]
        pick, pick_c = prob[0:16, 0:1024], prob[0:16, 1024:1536]
        spread = tiles(0, 8, T)
        spread_c = tiles(4096, 4, CTX)

        def pe_second(pe, me, claim, all_read, mm, weights, project, project_tokens, sum_squares, attention, unit):
            def project2(b, src, reader="act"):
                claim(b, reader)
                claim(b + 1, reader)
                w = weights()
                for s in range(2):
                    for k in range(KT):
                        ins = mm(banks[b + s][:, 0:(T, CTX)[s]], w[:, k, :], src[:, k, SPANS[s]], k == 0, k == KT - 1)
                        if s == 0 and k == 0:
                            ins.then_inc(w_turn, 1)
                    ins.then_inc(full_for_act if reader == "act" else full_for_dve, 1)

            def tokens2(b, src):
                claim(b, "act")
                claim(b + 1, "act")
                w = weights()
                for j in range(6):
                    for k in range(KT):
                        ins = mm(banks[b + j // 4][:, j % 4 * P:(j % 4 + 1) * P], src[:, k, j * P:(j + 1) * P],
                                 w[:, k, :], k == 0, k == KT - 1)
                        if j == 0 and k == 0:
                            ins.then_inc(w_turn, 1)
                    if j in (3, 5):
                        ins.then_inc(full_for_act, 1)

            def norms(both=True):
                sum_squares(4, lambda k: h[:, k, 0:T], T)
                if both:
                    sum_squares(5, lambda k: h[:, k, T:ALL], CTX)
                pe.wait_ge(operand_ready, me.nth(operand_ready))

            def hgrn(l):
                pe.wait_ge(operand_ready, me.nth(operand_ready))
                for p in range(HG_PAIRS):
                    for d in range(2):
                        pe.wait_ge(operand_ready, me.nth(operand_ready))
                        for s in range(2):
                            claim(4 + s, "act")
                            for c in range(4 * s, min(6, 4 * s + 4)):
                                ins = nc.tensor.transpose(banks[4 + s][:, c % 4 * P:(c % 4 + 1) * P],
                                                          k_exp[:, c * P:(c + 1) * P], ident)
                            ins.then_inc(full_for_act, 1)
                        all_read("act")
                        pe.wait_ge(scaled_ready, me.nth(scaled_ready))
                        for ci in range(N_CH + 1):
                            if ci < N_CH:
                                c = FLOW[d][ci]
                                cs = slice(c * P, (c + 1) * P)
                                for hh in range(2 if wanted(l, c) else 0):
                                    r = slice(hh * 64, hh * 64 + 64)
                                    claim(2 * hh, "dve")
                                    claim(2 * hh + 1, "dve")
                                    for n in range(8):
                                        a, bb = ((scaled[n][r, cs], scaled[n][r, cs]) if n < 7 else
                                                 (hg_z[r, 3 * d + p, cs], hg_q[r, p, cs]))
                                        ins = mm(banks[2 * hh + n // 4][:, n % 4 * P:(n % 4 + 1) * P], a, bb, True, True)
                                    ins.then_inc(full_for_dve, 1)
                                claim(6 + ci % 2, "state")
                                mm(banks[6 + ci % 2][:, 0:P], k_tok[:, cs], hg_v[:, c, p * P:(p + 1) * P], True,
                                   True).then_inc(full_for_dve, 1)
                            if ci >= 1:
                                c = FLOW[d][ci - 1]
                                cs = slice(c * P, (c + 1) * P)
                                b = 4 + (ci - 1) % 2
                                if not wanted(l, c):
                                    if ci >= 2:
                                        me.nth(state_ready)
                                    continue
                                claim(b, "dve")
                                if ci >= 2:
                                    pe.wait_ge(state_ready, me.nth(state_ready))
                                    mm(banks[b][:, 0:P], state[:, :], q_exp[:, cs], True, False)
                                for hh in range(2):
                                    pe.wait_ge(scores_ready, me.nth(scores_ready))
                                    at = ((ci - 1) % 2 * 2 + hh) * P
                                    ins = mm(banks[b][hh * 64:hh * 64 + 64, 0:P],
                                             hg_v[:, c, p * P + hh * 64:p * P + hh * 64 + 64], sums_st[:, at:at + P],
                                             ci == 1, True)
                                ins.then_inc(full_for_dve, 1)
                        me.nth(state_ready)
                    pe.wait_ge(squares_ready, me.nth(squares_ready))
                    for s in range(2):
                        claim(4 + s, "dve")
                        mm(banks[4 + s][:, 0:(T, CTX)[s]], cst(C_HEADS), probT[:, SPANS[s]], True,
                           True).then_inc(full_for_dve, 1)

            def experts(both):
                n_tok = 6 if both else 4
                claim(0, "dve")
                w = weights()
                for j in range(n_tok):
                    for k in range(KT):
                        ins = mm(banks[0][:, j * 16:j * 16 + 16], h[:, k, j * P:(j + 1) * P], w[:, k, 0:16],
                                 k == 0, k == KT - 1)
                        if j == 0 and k == 0:
                            ins.then_inc(w_turn, 1)
                ins.then_inc(full_for_dve, 1)
                for j in range(n_tok):
                    for g in range(2):
                        b = 4 + (2 * j + g) % 4
                        claim(b, "act")
                        for k in range(4):
                            ins = nc.tensor.transpose(banks[b][:, k * P:(k + 1) * P], h[:, 4 * g + k, j * P:(j + 1) * P],
                                                      ident)
                        ins.then_inc(full_for_act, 1)
                pe.wait_ge(operand_ready, me.nth(operand_ready))
                for s in range(1 + both):
                    claim(s, "dve")
                    for j in range(4 * s, min(6, 4 * s + 4)):
                        ins = nc.tensor.transpose(banks[s][0:16, j % 4 * P:(j % 4 + 1) * P], aff[:, j * 16:j * 16 + 16],
                                                  ident)
                    ins.then_inc(full_for_dve, 1)
                pe.wait_ge(operand_ready, me.nth(operand_ready))
                claim(2, "dve")
                for j in range(n_tok):
                    ins = mm(banks[2][:, j * 16:j * 16 + 16], ranks[:, j * P:(j + 1) * P], const[0:16, 0:16], True, True)
                ins.then_inc(full_for_dve, 1)
                all_read("act")

                def gather():
                    pe.wait_ge(one_hot_ready, me.nth(one_hot_ready))
                    for n in range(6 if both else 4):
                        claim(n % 2, "act")
                        for k in range(4):
                            ks = slice((4 * (n % 2) + k) * P, (4 * (n % 2) + k + 1) * P)
                            o = banks[n % 2][:, k * P:(k + 1) * P]
                            if n < 4:
                                pair = slice(n // 2 * 2 * CAP, (n // 2 + 1) * 2 * CAP)
                                for j in range(4):
                                    ins = mm(o, h_tok[:, j, ks], one_hot[:, j, pair], j == 0, j == 3)
                            else:
                                for j in range(2):
                                    ins = mm(o, h_tok[:, 4 + j, ks], one_hot_c[:, j, :], j == 0, j == 1)
                        ins.then_inc(full_for_act, 1)

                gather()
                for e in range(N_EXPERTS):
                    if e % QUAD == 0:
                        gathered_at = me.freed["act"]
                        pe.wait_ge(freed_by_act, gathered_at)
                    xg = gathered[e % QUAD // 2][:, e % 2]
                    for m in range(2):
                        claim(2 + m, ("act", "dve")[m])
                        for n in range(4):
                            w = weights()
                            for k in range(KT):
                                ins = mm(banks[2 + m][:, n * SLOTS:(n + 1) * SLOTS], w[:, k, :], xg[:, k, :],
                                         k == 0, k == KT - 1)
                                if k == 0:
                                    ins.then_inc(w_turn, 1)
                        ins.then_inc((full_for_act, full_for_dve)[m], 1)
                    if e % QUAD == QUAD - 1 and e + 1 < N_EXPERTS:
                        gather()
                    pe.wait_ge(operand_ready, me.nth(operand_ready))
                    hid = hidden[e % 2].rearrange("p (k s) -> p k s", k=4)
                    for n in range(4):
                        b = 4 + (2 * e + n // 2) % 4
                        if n % 2 == 0:
                            claim(b, "act")
                        w = weights(4)
                        for k in range(4):
                            ins = mm(banks[b][0:SLOTS, n % 2 * 256:n % 2 * 256 + 256], hid[:, k, :], w[:, k, :],
                                     k == 0, k == 3)
                            if k == 0:
                                ins.then_inc(w_turn, 1)
                        if n % 2:
                            ins.then_inc(full_for_act, 1)
                all_read("act")
                for n in range(12 if both else 8):
                    b = 4 * (n % 2)
                    for m, src in enumerate((ranks, vals)):
                        claim(b + m, "dve")
                        if n < 8:
                            ins = mm(banks[b + m][:, :], pick[:, n * P:(n + 1) * P], src[:, 0:T], True, True)
                        else:
                            ins = mm(banks[b + m][:, 0:CTX], pick_c[:, (n - 8) * P:(n - 7) * P], src[:, T:ALL], True, True)
                    ins.then_inc(full_for_dve, 1)
                pe.wait_ge(operand_ready, me.nth(operand_ready))
                for f in range(KT):
                    fs = slice(f * P, (f + 1) * P)
                    for s, (o, sp_, n) in enumerate(((out_e, spread, 8), (out_c, spread_c, 4))[:1 + both]):
                        b = 2 * (f % 2) + s
                        claim(b, "dve")
                        for m in range(n):
                            ins = mm(banks[b][:, 0:(T, CTX)[s]], o[:, m, fs], sp_[:, m, :], m == 0, m == n - 1)
                        ins.then_inc(full_for_dve, 1)

            def second_layer(l):
                pe.wait_ge(act_output2, me.nth(act_output2))
                for n in range(48):
                    b = n // 4 % 4
                    if n % 4 == 0:
                        claim(b, "dve")
                    w = weights()
                    for k in range(KT):
                        ins = mm(banks[b][0:2, n % 4 * P:(n % 4 + 1) * P], csil[:, 2 * k:2 * k + 2], w[:, k, :],
                                 k == 0, k == KT - 1)
                        if k == 0:
                            ins.then_inc(w_turn, 1)
                    if n % 4 == 3:
                        ins.then_inc(full_for_dve, 1)
                all_read("dve")
                claim(6, None)
                for n in range(48):
                    ins = nc.tensor.transpose(banks[6][:, 2 * n:2 * n + 2], mod_rows[:, n * P:(n + 1) * P],
                                              const[0:2, C_IDENT:C_IDENT + 2])
                ins.then_inc(full_for_dve, 1)
                norms()
                for n in range(6):
                    project2((n % 2) * 2, h, "dve")
                for n in range(9):
                    (tokens2 if n >= 6 else project2)((n % 2) * 2, h)
                for n in range(6):
                    if n % 2 == 0:
                        pe.wait_ge(squares_ready, me.nth(squares_ready))
                    for s in range(2):
                        b = (n % 2) * 2 + s
                        claim(b, "dve")
                        mm(banks[b][:, 0:(T, CTX)[s]], cst(C_HEADS), head_sq[:, n, SPANS[s]], True,
                           True).then_inc(full_for_dve, 1)
                pe.wait_ge(operand_ready, me.nth(operand_ready))
                for n in range(6):
                    for s in range(2):
                        b = (n % 2) * 2 + s
                        claim(b, "dve")
                        mm(banks[b][:, 0:(T, CTX)[s]], cst(C_ROT2), (na_q if n < 3 else na_k)[:, n % 3, SPANS[s]],
                           True, True).then_inc(full_for_dve, 1)
                pe.wait_ge(operand_ready, me.nth(operand_ready))
                attention(na_units())
                if need_ctx(l):
                    attention(ctx_units())
                for n in range(15):
                    (tokens2 if 9 <= n < 12 else project2)((n % 2) * 2, h)
                hgrn(l)
                pe.wait_ge(operand_ready, me.nth(operand_ready))
                for n in range(KT):
                    if need_ctx(l):
                        project2((n % 2) * 2, mix, "dve")
                    else:
                        project((n % 2) * 2, lambda k: mix[:, k, 0:T], T, "dve")
                norms(need_ctx(l))
                experts(need_ctx(l))

            sum_squares(0, lambda k: h[:, k, 0:T], T)
            pe.wait_ge(operand_ready, me.nth(operand_ready))
            pe.wait_ge(ctx_in, 32)
            for l in range(DEPTH):
                second_layer(l)

        def act_second(act, me, A, bank_full, evacuate, squares, roots, attention):
            def norms(both=True):
                squares(h[:, :, 0:T], x[:, :, 0:T])
                if both:
                    squares(h[:, :, T:ALL], x[:, :, T:ALL])
                roots(rstd[:, 0:T])
                if both:
                    roots(rstd[:, T:ALL])

            def await_input():
                act.wait_ge(act_input, me.nth(act_input))

            def evacuate2(b, dst, func=ACT.Copy, **kw):
                for s in range(2):
                    evacuate(dst[:, SPANS[s]], banks[b + s][:, 0:(T, CTX)[s]], func, **kw)

            def evacuate_tokens(b, dst, n):
                for s in range(2):
                    m = (4, 2)[s]
                    evacuate(dst[:, 4 * s:4 * s + m, n * P:(n + 1) * P],
                             banks[b + s][:, 0:m * P].rearrange("p (j n) -> p j n", j=m))

            def hgrn(l):
                await_input()
                lb = lbv[:, 0:6]
                me.link(A(lbv[:, 6:12], lb, ACT.Abs))
                me.link(A(lbv[:, 6:12], lbv[:, 6:12], ACT.Exp, scale=-1.0))
                e = hg_a
                me.link(A(e[:, :, :], hg_z[:, :, :], ACT.Abs))
                me.link(A(e[:, :, :], e[:, :, :], ACT.Exp, scale=-1.0))
                me.link(A(lbv[:, 6:12], lbv[:, 6:12], ACT.Ln, bias=1.0))
                me.link(A(e[:, :, :], e[:, :, :], ACT.Ln, bias=1.0), act_output)
                await_input()
                me.link(A(hg_z[:, :, :], hg_z[:, :, :], ACT.Exp), act_output)
                for d in range(2):
                    await_input()
                    me.link(A(hg_tmp[:, :, :], hg_tmp[:, :, :], ACT.Abs))
                    me.link(A(hg_tmp[:, :, :], hg_tmp[:, :, :], ACT.Exp, scale=-1.0))
                    me.link(A(hg_tmp[:, :, :], hg_tmp[:, :, :], ACT.Ln, bias=1.0), act_output)
                for p in range(HG_PAIRS):
                    for d in range(2):
                        await_input()
                        me.link(A(q_exp, hg_a[:, 3 * d + p, :], ACT.Exp), wait=False)
                        me.link(A(last_dec, last_sum, ACT.Exp), wait=False)
                        me.link(A(k_exp, k_exp, ACT.Exp), act_output)
                        for n in range(7):
                            await_input()
                            me.link(A(scaled[n], scaled[n], ACT.Exp), act_output, wait=False)
                        for s in range(2):
                            m = (4, 2)[s]
                            evacuate(k_tok[:, 4 * s * P:(4 * s + m) * P], banks[4 + s][:, 0:m * P])
                    await_input()
                    me.link(A(probT[:, 0:ALL], acc_o[:, :], ACT.Square), squares_ready)
                    roots(rstd[:, :])

            def experts(both):
                n_tok = 6 if both else 4
                for j in range(n_tok):
                    for g in range(2):
                        evacuate(h_tok[:, j, g * 512:(g + 1) * 512], banks[4 + (2 * j + g) % 4][:, :])
                await_input()
                me.link(A(aff[:, 0:n_tok * 16], aff[:, 0:n_tok * 16], ACT.Exp), act_output)

                def gathered_out():
                    for n in range(6 if both else 4):
                        bank_full()
                        g = slice(4 * (n % 2), 4 * (n % 2) + 4)
                        bank = banks[n % 2][:, :]
                        if n < 4:
                            me.link(A(gathered[n // 2][:, :, g, 0:CAP].rearrange("p e k s -> p k e s"),
                                      bank.rearrange("p (k e s) -> p k e s", k=4, e=2), ACT.Copy), freed_by_act, wait=False)
                        else:
                            quad = bank.rearrange("p (k e s) -> p k e s", k=4, e=4)
                            for pair in range(2):
                                me.link(A(gathered[pair][:, :, g, CAP:SLOTS].rearrange("p e k s -> p k e s"),
                                          quad[:, :, 2 * pair:2 * pair + 2, :], ACT.Copy),
                                        freed_by_act if pair else None, wait=False)

                gathered_out()
                for e in range(N_EXPERTS):
                    bank_full()
                    me.link(A(silu_g[e % 2], banks[2][:, 0:384], ACT.Silu), freed_by_act)
                    me.notify(act_output)
                    if e % QUAD == QUAD - 1 and e + 1 < N_EXPERTS:
                        gathered_out()
                    for n in range(2):
                        b = 4 + (2 * e + n) % 4
                        bank_full()
                        cols = slice(n * 512, (n + 1) * 512)
                        if both:
                            me.link(A(out_c[32 * (e % 4):32 * (e % 4) + 32, e // 4, cols], banks[b][CAP:SLOTS, :],
                                      ACT.Copy), wait=False)
                        me.link(A(out_e[64 * (e % 2):64 * (e % 2) + 64, e // 2, cols], banks[b][0:CAP, :], ACT.Copy),
                                freed_by_act, wait=False)

            def second_layer(l):
                me.link(A(csil, par2(l, B_COND, 16), ACT.Silu), act_output2, wait=False)
                await_input()
                norms()
                await_input()
                for n in range(9):
                    b = (n % 2) * 2
                    if n < 6:
                        evacuate2(b, (na_q if n < 3 else na_k)[:, n % 3, :])
                    else:
                        evacuate_tokens(b, na_v, n - 6)
                me.eng.wait_ge(freed_by_act, me.done["freed_by_act"])
                for n in range(3):
                    src = (na_q, na_k)[n * 2 // 3]
                    me.link(A(head_sq[:, 2 * n, :], (na_q if 2 * n < 3 else na_k)[:, 2 * n % 3, :], ACT.Square), wait=False)
                    me.link(A(head_sq[:, 2 * n + 1, :], (na_q if 2 * n + 1 < 3 else na_k)[:, (2 * n + 1) % 3, :],
                              ACT.Square), squares_ready, wait=False)
                roots(head_sq[:, :, :])
                attention(na_units())
                if need_ctx(l):
                    attention(ctx_units())
                for n in range(15):
                    b = (n % 2) * 2
                    if n < 3:
                        evacuate2(b, hg_q[:, n, :], scale=HD ** -0.5)
                    elif n < 9:
                        evacuate2(b, hg_z[:, n - 3, :])
                    elif n < 12:
                        evacuate_tokens(b, hg_v, n - 9)
                    else:
                        evacuate2(b, mix[:, 3 + n - 12, :], ACT.Silu)
                me.eng.wait_ge(freed_by_act, me.done["freed_by_act"])
                hgrn(l)
                await_input()
                norms(need_ctx(l))
                experts(need_ctx(l))

            await_input()
            squares(h[:, :, 0:T], x[:, :, 0:T])
            roots(rstd[:, 0:T])
            act.wait_ge(ctx_in, 32)
            for l in range(DEPTH):
                second_layer(l)

        def dve_second(dve, me, V, bank_full, await_, inverse_deviation, norm, attention):
            def modulated(which, shift, both=True):
                for s in range(1 + both):
                    inverse_deviation(4 + s, SPANS[s])
                    for k in range(KT):
                        c = (which * KT + k) * 2 + s
                        o = h[:, k, SPANS[s]]
                        me.link(V.scalar_tensor_tensor(out=o, in0=x[:, k, SPANS[s]], scalar=mod_a[:, c:c + 1],
                                                       in1=rstd[:, SPANS[s]], op0=ALU.mult, op1=ALU.mult))
                        me.link(V.tensor_scalar(o, o, modc(shift, k, s), None, ALU.add))
                me.notify(operand_ready)

            def add_gated(gate, order, both):
                for n in range(KT):
                    for s in range(1 + both):
                        bank_full()
                        o = x[:, n, SPANS[s]]
                        me.link(V.scalar_tensor_tensor(out=o, in0=banks[order(n) + s][:, 0:(T, CTX)[s]],
                                                       scalar=modc(gate, n, s), in1=o, op0=ALU.mult, op1=ALU.add),
                                freed_by_dve)

            def conv(l):
                z = [flat(n * (ALL + 4), ALL + 4) for n in range(2)]
                at = (1, T + 3)
                for n in range(2):
                    me.link(V.memset(z[n], 0.0))
                for n in range(6):
                    for s in range(2):
                        bank = banks[(n % 2) * 2 + s][:, 0:(T, CTX)[s]]
                        zz = z[n % 2][:, at[s]:at[s] + (T, CTX)[s]]
                        bank_full()
                        if n < 2:
                            me.link(V.tensor_copy(zz, bank), freed_by_dve)
                        elif n < 4:
                            me.link(V.tensor_tensor(zz, zz, bank, ALU.mult), freed_by_dve)
                        else:
                            o = mix[:, 6 + n - 4, SPANS[s]]
                            for j in range(3):
                                src = z[n % 2][:, at[s] + j - 1:at[s] + j - 1 + (T, CTX)[s]]
                                wc = par2(l, B_CONV + 3 * (n - 4) + j)
                                if j == 0:
                                    me.link(V.tensor_scalar(o, src, wc, None, ALU.mult))
                                else:
                                    me.link(V.scalar_tensor_tensor(out=o, in0=src, scalar=wc, in1=o, op0=ALU.mult,
                                                                   op1=ALU.add))
                            me.link(V.tensor_tensor(o, o, bank, ALU.mult), freed_by_dve)
                me.notify(act_input)

            def head_norms(l):
                for n in range(6):
                    for s in range(2):
                        bank_full()
                        me.link(V.tensor_scalar(head_sq[:, n, SPANS[s]], banks[(n % 2) * 2 + s][:, 0:(T, CTX)[s]], 1.0 / HD,
                                                EPS, ALU.mult, ALU.add), freed_by_dve)
                me.notify(variance_ready)
                dve.wait_ge(table_in, 16 * (l + 1))
                m = cst(C_COLMASK, GRID).rearrange("p (a c) -> p a c", a=1).to_broadcast([P, NA_HEADS * 14, GRID])
                bt = bias_table.rearrange("p (a c) -> p a c", c=GRID)
                me.link(V.tensor_tensor(bt, bt, m, ALU.add))
                await_(root_ready)
                me.link(V.reciprocal(head_sq[:, :, :], head_sq[:, :, :]))
                for n in range(6):
                    t = (na_q if n < 3 else na_k)[:, n % 3, :]
                    me.link(V.scalar_tensor_tensor(out=t, in0=t, scalar=par2(l, B_QN if n < 3 else B_KN),
                                                   in1=head_sq[:, n, :], op0=ALU.mult, op1=ALU.mult))
                me.notify(operand_ready)
                cos, sin = cst(C_TAB, ALL), cst(C_TAB + ALL, ALL)
                for n in range(6):
                    for s in range(2):
                        t = (na_q if n < 3 else na_k)[:, n % 3, SPANS[s]]
                        tmp = acc_o[:, SPANS[s]]
                        bank_full()
                        me.link(V.tensor_tensor(tmp, banks[(n % 2) * 2 + s][:, 0:(T, CTX)[s]], sin[:, SPANS[s]], ALU.mult),
                                freed_by_dve)
                        me.link(V.tensor_tensor(t, t, cos[:, SPANS[s]], ALU.mult))
                        me.link(V.tensor_tensor(t, t, tmp, ALU.add))
                me.notify(operand_ready)

            def gates(l):
                lb, lb1 = lbv[:, 0:6], lbv[:, 6:12]
                diff2 = lambda d, m: par2(l, B_LB + 6 * d + 3 * m, 3)
                for d in range(2):
                    me.link(V.tensor_tensor(lb[:, 3 * d:3 * d + 3], diff2(d, 1), diff2(d, 0), ALU.subtract))
                me.notify(act_input)
                await_(act_output)
                if l == 0:
                    me.link(V.memset(lb, NEG))
                    me.link(V.memset(lb1, 0.0))
                else:
                    me.link(V.scalar_tensor_tensor(out=lb1, in0=lb, scalar=0.0, in1=lb1, op0=ALU.min, op1=ALU.subtract))
                    me.link(V.tensor_tensor(last_sum, lb1, lb, ALU.subtract))
                    me.link(V.tensor_copy(lb, lb1))
                    me.link(V.tensor_copy(lb1, last_sum))
                b = hg_a
                me.link(V.scalar_tensor_tensor(out=b[:, :, :], in0=hg_z[:, :, :], scalar=0.0, in1=b[:, :, :],
                                               op0=ALU.min, op1=ALU.subtract))
                for n in range(6):
                    me.link(V.tensor_scalar(b[:, n, :], b[:, n, :], lb1[:, n:n + 1], None, ALU.add))
                me.link(V.tensor_tensor(hg_z[:, :, :], b[:, :, :], hg_z[:, :, :], ALU.subtract), act_input, wait=False)
                await_(act_output)
                for d in range(2):
                    for n in range(3):
                        me.link(V.tensor_scalar(hg_tmp[:, n, :], b[:, 3 * d + n, :], lb[:, 3 * d + n:3 * d + n + 1], None,
                                                ALU.subtract))
                    me.notify(act_input)
                    await_(act_output)
                    for n in range(3):
                        t = b[:, 3 * d + n, :]
                        me.link(V.scalar_tensor_tensor(out=t, in0=t, scalar=lb[:, 3 * d + n:3 * d + n + 1],
                                                       in1=hg_tmp[:, n, :], op0=ALU.max, op1=ALU.add))
                        for c in range(N_CH):
                            v = t[:, c * P:(c + 1) * P]
                            if d == 1:
                                v = v[:, ::-1]
                            me.link(V.tensor_tensor_scan(v, v, v, 0.0, ALU.add, ALU.bypass), wait=False)
                        dve.wait_ge(dve_step, me.done["dve_step"])
                me.notify(operand_ready)

            def hgrn(l):
                gates(l)
                for p in range(HG_PAIRS):
                    for d in range(2):
                        a = hg_a[:, 3 * d + p, :]
                        q, k = hg_q[:, p, :], hg_z[:, 3 * d + p, :]
                        ends = a.rearrange("p (c n) -> p c n", c=N_CH)[:, :, P - 1 if d == 0 else 0]
                        me.link(V.tensor_copy(last_sum, ends))
                        by = lambda v: v.rearrange("p (c n) -> p c n", c=N_CH)
                        me.link(V.tensor_tensor(by(k_exp), last_sum.rearrange("p (c n) -> p c n", n=1).to_broadcast([P, N_CH, P]),
                                                by(a), ALU.subtract), act_input)

                        def halves(v, m):
                            w = v.rearrange("p (b two m) -> p b two m", two=2, m=m)
                            return w[:, :, d, :], w[:, :, 1 - d, :]

                        for n, m in enumerate(LEVELS):
                            nb = ALL // (2 * m)
                            early, late = halves(a, m)
                            edge = early[:, :, m - 1 if d == 0 else 0:m if d == 0 else 1].to_broadcast([P, nb, m])
                            x_early, x_late = halves(scaled[n], m)
                            me.link(V.tensor_tensor(x_early, edge, early, ALU.subtract), wait=False)
                            me.link(V.tensor_tensor(x_late, late, edge, ALU.subtract), act_input, wait=False)
                        await_(act_output)
                        me.link(V.tensor_tensor(q_exp, q_exp, q, ALU.mult))
                        me.link(V.tensor_tensor(k_exp, k_exp, k, ALU.mult), operand_ready)
                        for n, m in enumerate(LEVELS):
                            await_(act_output)
                            x_early, x_late = halves(scaled[n], m)
                            k_early, _ = halves(k, m)
                            _, q_late = halves(q, m)
                            me.link(V.tensor_tensor(x_early, x_early, k_early, ALU.mult), wait=False)
                            me.link(V.tensor_tensor(x_late, x_late, q_late, ALU.mult), wait=n == 6)
                        me.notify(scaled_ready)
                        masks = cst(C_LEVEL if d == 0 else C_LEVEL_BACK, 1024)
                        for ci in range(N_CH + 1):
                            if ci < N_CH:
                                for hh in range(2 if wanted(l, FLOW[d][ci]) else 0):
                                    bank_full()
                                    pr = products[hh]
                                    for g in range(2):
                                        me.link(V.tensor_tensor(pr[:, g * 512:(g + 1) * 512], banks[2 * hh + g][:, :],
                                                                masks[:, g * 512:(g + 1) * 512], ALU.mult), freed_by_dve)
                                    at = (ci % 2 * 2 + hh) * P
                                    me.link(V.tensor_reduce(sums_st[:, at:at + P], pr.rearrange("p (l t) -> p t l", l=8),
                                                            AX.X, ALU.add), scores_ready, wait=False)
                                bank_full()
                            if ci >= 1:
                                c = FLOW[d][ci - 1]
                                o, bank = acc_o[:, c * P:(c + 1) * P], banks[4 + (ci - 1) % 2][:, 0:P]
                                if wanted(l, c):
                                    bank_full()
                                    if d == 0:
                                        me.link(V.tensor_copy(o, bank), freed_by_dve)
                                    else:
                                        me.link(V.tensor_tensor(o, o, bank, ALU.add), freed_by_dve)
                                sb_ = banks[6 + (ci - 1) % 2][:, 0:P]
                                if ci == 1:
                                    me.link(V.tensor_tensor(state, sb_, cst(C_HEADS), ALU.mult), state_ready)
                                else:
                                    me.link(V.tensor_tensor(state_new, sb_, cst(C_HEADS), ALU.mult))
                                    me.link(V.scalar_tensor_tensor(out=state, in0=state, scalar=last_dec[:, c:c + 1],
                                                                   in1=state_new, op0=ALU.mult, op1=ALU.add), state_ready)
                    me.notify(act_input)
                    for s in range(2):
                        bank_full()
                        me.link(V.tensor_scalar(rstd[:, SPANS[s]], banks[4 + s][:, 0:(T, CTX)[s]], 1.0 / HD, EPS, ALU.mult,
                                                ALU.add), freed_by_dve)
                    me.notify(variance_ready)
                    await_(root_ready)
                    me.link(V.reciprocal(rstd[:, :], rstd[:, :]))
                    me.link(V.scalar_tensor_tensor(out=acc_o[:, :], in0=acc_o[:, :], scalar=par2(l, B_HGN), in1=rstd[:, :],
                                                   op0=ALU.mult, op1=ALU.mult))
                    me.link(V.tensor_tensor(mix[:, 3 + p, :], mix[:, 3 + p, :], acc_o[:, :], ALU.mult))
                me.notify(operand_ready)

            def choose(both):
                bank_full()
                n_tok = 6 if both else 4
                v3 = lambda v: v.rearrange("p (j e) -> p j e", j=6)[:, 0:n_tok, :]
                b3 = lambda v: v[:, 0:n_tok].rearrange("p (j e) -> p j e", e=1).to_broadcast([P, n_tok, 16])
                me.link(V.reduce_max(row_max[:, 0:n_tok], v3(banks[0][:, 0:96]), AX.X))
                me.link(V.tensor_tensor(v3(aff), v3(banks[0][:, 0:96]), b3(row_max), ALU.subtract), freed_by_dve)
                me.notify(act_input)
                await_(act_output)
                me.link(V.reduce_sum(row_sum[:, 0:n_tok], v3(aff), AX.X))
                me.link(V.reciprocal(row_sum[:, 0:n_tok], row_sum[:, 0:n_tok]))
                me.link(V.tensor_tensor(v3(aff), v3(aff), b3(row_sum), ALU.mult), operand_ready)
                for s in range(1 + both):
                    bank_full()
                    me.link(V.tensor_copy(aff_t[:, SPANS[s]], banks[s][0:16, 0:(T, CTX)[s]]), freed_by_dve)
                w = slice(0, ALL if both else T)
                me.link(V.tensor_copy(left[:, w], aff_t[:, w]))
                for s, cap in enumerate((CAP, CAP_CTX)[:1 + both]):
                    for _ in range(cap // 8):
                        me.link(V.max(top8, left[:, SPANS[s]]))
                        me.link(V.match_replace(left[:, SPANS[s]], top8, left[:, SPANS[s]], -1.0))
                me.link(V.tensor_scalar(left[:, w], left[:, w], 0.0, None, ALU.is_lt))
                me.link(V.tensor_tensor(vals[:, w], aff_t[:, w], left[:, w], ALU.mult))
                for s in range(1 + both):
                    me.link(V.tensor_tensor_scan(ranks[:, SPANS[s]], left[:, SPANS[s]], left[:, SPANS[s]], 0.0,
                                                 ALU.add, ALU.bypass))
                for o, cap in ((pick, CAP), (pick_c, CAP_CTX))[:1 + both]:
                    me.link(V.tensor_copy(o.rearrange("p (e s) -> p e s", e=16),
                                          const[0:16, 0:16].rearrange("p (e s) -> p e s", s=1).to_broadcast([16, 16, cap])))
                me.link(V.tensor_tensor(ranks[:, w], ranks[:, w], left[:, w], ALU.mult), operand_ready)
                bank_full()
                me.link(V.tensor_copy(rank_tok[:, 0:n_tok * 16], banks[2][:, 0:n_tok * 16]), freed_by_dve)

            def one_hots(q, both):
                for o, j0, m, cap in ((one_hot, 0, 4, CAP), (one_hot_c, 4, 2, CAP_CTX))[:1 + both]:
                    slots = cst(C_SLOTROW, cap).rearrange("p (a b n) -> p a b n", a=1, b=1).to_broadcast([P, m, QUAD, cap])
                    rank = rank_tok.rearrange("p (j e n) -> p j e n", j=6, n=1)[:, j0:j0 + m, QUAD * q:QUAD * q + QUAD]
                    me.link(V.tensor_tensor(o[:, :, :].rearrange("p j (e n) -> p j e n", e=QUAD), slots,
                                            rank.to_broadcast([P, m, QUAD, cap]), ALU.is_equal),
                            one_hot_ready if j0 or not both else None, wait=False)

            def experts(both):
                choose(both)
                one_hots(0, both)
                for e in range(N_EXPERTS):
                    await_(act_output)
                    bank_full()
                    me.link(V.tensor_tensor(hidden[e % 2], silu_g[e % 2], banks[3][:, 0:384], ALU.mult), freed_by_dve)
                    me.notify(operand_ready)
                    if e % QUAD == 0 and e + QUAD < N_EXPERTS:
                        one_hots(e // QUAD + 1, both)
                for n in range(12 if both else 8):
                    b = 4 * (n % 2)
                    w = T if n < 8 else CTX
                    o = spread[:, n, :] if n < 8 else spread_c[:, n - 8, :]
                    col = const[:, C_SLOT + n // 8:C_SLOT + n // 8 + 1]
                    bank_full()
                    me.link(V.tensor_copy(acc_o[:, 0:w], banks[b + 1][:, 0:w]))
                    me.link(V.scalar_tensor_tensor(out=o, in0=banks[b][:, 0:w], scalar=col, in1=acc_o[:, 0:w],
                                                   op0=ALU.is_equal, op1=ALU.mult), freed_by_dve)
                    me.notify(freed_by_dve)
                me.notify(operand_ready)
                add_gated(5, lambda n: 2 * (n % 2), both)

            def second_layer(l):
                me.notify(table_room)
                for n in range(12):
                    bank_full()
                    me.link(V.tensor_copy(mod_rows[:, n * T:(n + 1) * T], banks[n % 4][0:2, :]), freed_by_dve, wait=False)
                bank_full()
                b3 = lambda v, k: v.rearrange("p (k s) -> p k s", k=k)
                me.link(V.tensor_tensor(b3(modv, 48), b3(banks[6][:, 0:96], 48),
                                        par2(l, B_MOD, 48).rearrange("p (k s) -> p k s", s=1).to_broadcast([P, 48, 2]), ALU.add))
                for n, (m, w) in enumerate(((1, B_N1), (4, B_N2))):
                    o = mod_a[:, n * 16:n * 16 + 16]
                    me.link(V.scalar_tensor_tensor(out=b3(o, 8), in0=b3(modv[:, m * 16:m * 16 + 16], 8), scalar=1.0,
                                                   in1=par2(l, w, 8).rearrange("p (k s) -> p k s", s=1).to_broadcast([P, 8, 2]),
                                                   op0=ALU.add, op1=ALU.mult))
                modulated(0, 0)
                conv(l)
                head_norms(l)
                attention(na_units())
                if need_ctx(l):
                    attention(ctx_units())
                hgrn(l)
                add_gated(2, lambda n: (n % 2) * 2, need_ctx(l))
                me.notify(act_input)
                modulated(1, 3, need_ctx(l))
                experts(need_ctx(l))
                if l < DEPTH - 1:
                    me.notify(act_input)
                else:
                    me.notify(result_ready)

            norm(0, x[:, :, 0:T], x[:, :, 0:T], lambda k: par1(0, A_FINAL + k), slice(0, T))
            me.notify(act_input)
            me.notify(operand_ready)
            dve.wait_ge(ctx_in, 32)
            for l in range(DEPTH):
                second_layer(l)

        @block.tensor
        def _(pe):
            me = Engine(pe, None)
            last_reader, freed = {}, {"act": 0, "dve": 0, "exp": 0, "raw": 0, "state": 0}
            me.freed = freed
            free_sem = {"act": freed_by_act, "dve": freed_by_dve, "exp": exp_ready, "raw": raw_ready, "state": state_ready}
            full_sem = {"act": full_for_act, "dve": full_for_dve}
            unit = [0]

            def claim(b, freer):
                if b in last_reader:
                    pe.wait_ge(*last_reader.pop(b))
                if freer is None:
                    return
                freed[freer] += 1
                last_reader[b] = (free_sem[freer], freed[freer])

            def all_read(who):
                if freed[who]:
                    pe.wait_ge(free_sem[who], freed[who])

            def mm(o, a, b, first, last):
                return nc.tensor.matmul(o, a, b, start=first, stop=last, skip_group_check=True)

            def weights(kt=KT):
                n = unit[0]
                unit[0] += 1
                pe.wait_ge(w_loaded[n % RING], 16 * (n // RING + 1))
                return ring[:, n % RING * 1024:(n % RING + 1) * 1024].rearrange("p (k n) -> p k n", k=kt)

            def project(b, rhs, n, reader="act", pieces=1, freer=None):
                claim(b, freer or reader)
                for piece in range(pieces):
                    w = weights()
                    for k in range(KT):
                        ins = mm(banks[b][:, 0:n], w[:, k, :], rhs(piece * KT + k),
                                 piece == 0 and k == 0, piece == pieces - 1 and k == KT - 1)
                        if k == 0:
                            ins.then_inc(w_turn, 1)
                ins.then_inc(full_sem[reader], 1)

            def project_tokens(b, lhs, n, reader="act"):
                claim(b, reader)
                w = weights()
                for j in range(n):
                    for k in range(KT):
                        ins = mm(banks[b][:, j * P:(j + 1) * P], lhs(k, j), w[:, k, :], k == 0, k == KT - 1)
                        if j == 0 and k == 0:
                            ins.then_inc(w_turn, 1)
                ins.then_inc(full_sem[reader], 1)

            def sum_squares(b, tile, n, k_tiles=KT, what=C_ONES):
                claim(b, None)
                for k in range(k_tiles):
                    if k % 2 == 0:
                        pe.wait_ge(squares_ready, me.nth(squares_ready))
                    ins = mm(banks[b][:, 0:n], cst(what), tile(k), k == 0, k == k_tiles - 1)
                ins.then_inc(full_for_dve, 1)

            def in_pieces(n_units, per, rhs, lhs=None, token_major=()):
                for n in range(n_units):
                    b = 2 + n % 2
                    claim(b, None)
                    w = weights()
                    for piece in range(per):
                        if n in token_major:
                            steps = [(j, k) for j in range(CHUNKS * piece // per, CHUNKS * (piece + 1) // per)
                                     for k in range(KT)]
                        else:
                            steps = [(0, k) for k in range(KT * piece // per, KT * (piece + 1) // per)]
                        for j, k in steps:
                            if n in token_major:
                                ins = mm(banks[b][:, j * P:(j + 1) * P], lhs(k, j), w[:, k, :], k == 0, k == KT - 1)
                            else:
                                ins = mm(banks[b][:, :], w[:, k, :], rhs(k), k == 0, k == KT - 1)
                            if j == 0 and k == 0:
                                ins.then_inc(w_turn, 1)
                        if piece == per - 1:
                            ins.then_inc(full_for_act, 1)
                            claim(b, "act")
                        yield

            def attention(units, beside=None):
                us = list(units)
                out_n = 0
                group = 0
                for i in range(len(us) + 2):
                    if i < len(us):
                        u = us[i]
                        claimed = set()
                        for part in u["parts"]:
                            half, at, n, prods = part[:4]
                            b = 2 * half + i % 2
                            if b not in claimed:
                                claim(b, "dve" if u.get("bias") else "exp")
                                claimed.add(b)
                            extra = part[4] if len(part) > 4 else None
                            for j, (a, r) in enumerate(prods):
                                ins = mm(banks[b][:, at:at + n], a, r, j == 0,
                                         j == len(prods) - 1 and extra is None)
                            if extra:
                                ins = mm(banks[b][:, extra[2]:extra[2] + P], extra[0], extra[1], False, True)
                        ins.then_inc(full_for_dve, 1)
                    if 1 <= i <= len(us):
                        u = us[i - 1]
                        pe.wait_ge(prob_ready, me.nth(prob_ready))
                        nb = u["nk"] // P
                        for c in range(0, nb, 4):
                            b = 4 + (i - 1 + c // 4) % 2 if nb <= 4 else 4 + c // 4
                            claim(b, "act")
                            m = min(4, nb - c)
                            for j in range(m):
                                at = (i - 1) % 2 * ALL + (c + j) * P
                                ins = nc.tensor.transpose(banks[b][:, j * P:(j + 1) * P],
                                                          prob[:, at:at + P], ident)
                            ins.then_inc(full_for_act, 1)
                            u["ready_at"] = freed["act"]
                    if i >= 2:
                        u = us[i - 2]
                        pe.wait_ge(freed_by_act, u["ready_at"])
                        if group == 0:
                            for j in range(len(u["outs"])):
                                claim(6 + (out_n + j) % 2, "dve")
                        group = 1
                        for j, (_, rows, qi) in enumerate(u["outs"]):
                            o = banks[6 + (out_n + j) % 2][rows, qi * P:(qi + 1) * P]
                            wide = (rows.stop - rows.start)
                            for kb, v in enumerate(u["v"]):
                                at = (i - 2) % 2 * ALL + kb * P
                                ins = mm(o, v[:, j * wide:(j + 1) * wide] if len(u["outs"]) > 1 else v,
                                         probT[:, at:at + P], kb == 0, kb == len(u["v"]) - 1)
                        if u["closes"]:
                            ins.then_inc(full_for_dve, 1)
                            out_n += len(u["outs"])
                            group = 0
                    if beside is not None:
                        next(beside, None)
                for _ in beside or ():
                    pass

            def first_layer(l):
                hk = lambda k: h[:, k, 0:T]
                htok = lambda k, j: h[:, k, j * P:(j + 1) * P]
                sum_squares(0, hk, T)
                pe.wait_ge(operand_ready, me.nth(operand_ready))
                for n in range(10):
                    if n == 5:
                        project_tokens(n % 4, htok, CHUNKS)
                    else:
                        project(n % 4, hk, T)
                all_read("act")
                for n in range(5):
                    claim(n % 4, "dve")
                    at = n * T if n < 4 else 2048
                    mm(banks[n % 4][:, :], cst(C_ROT1), flat(at, T), True, True).then_inc(full_for_dve, 1)
                pe.wait_ge(operand_ready, me.nth(operand_ready))
                attention(swa_units(l), in_pieces(17, 2, hk, htok, range(9, 13)))
                all_read("act")
                pe.wait_ge(operand_ready, me.nth(operand_ready))
                attention(fox_units(), in_pieces(8, 4, hk))
                for n in range(12):
                    project(n % 4, hk, T, freer="raw")
                pe.wait_ge(operand_ready, me.nth(operand_ready))
                for c in range(CHUNKS):
                    for g in range(2):
                        b = (2 * c + g) % 4
                        claim(b, "act")
                        for j in range(4):
                            ins = nc.tensor.transpose(banks[b][:, j * P:(j + 1) * P],
                                                      xbc[:, 4 * g + j, c * P:(c + 1) * P], ident)
                        ins.then_inc(full_for_act, 1)
                for g in range(2):
                    claim(g, "act")
                    for c in range(CHUNKS):
                        ins = nc.tensor.transpose(banks[g][:, c * P:(c + 1) * P],
                                                  xbc[:, 8 + g, c * P:(c + 1) * P], ident)
                    ins.then_inc(full_for_act, 1)
                id16 = const[FD, C_IDENT + 32:C_IDENT + 48]
                claim(2, "dve")
                for c in range(CHUNKS):
                    cs = slice(c * P, (c + 1) * P)
                    mm(banks[2][:, c * 16:c * 16 + 16], gates[FD, cs], id16, True, True)
                    mm(banks[2][:, 64 + c * 16:80 + c * 16], acs[FD, cs], id16, True, True)
                    ins = mm(banks[2][:, 128 + c * 16:144 + c * 16],
                             acs[FD, (c + 1) * P - 1:(c + 1) * P].to_broadcast([16, P]), id16, True, True)
                ins.then_inc(full_for_dve, 1)
                for g in range(2):
                    b = (0, 3)[g]
                    claim(b, "dve")
                    for c in range(CHUNKS):
                        cs = slice(c * P, (c + 1) * P)
                        ins = mm(banks[b][:, cs], xbc[:, 8 + g, cs], xbc[:, 10 + g, cs], True, True)
                    ins.then_inc(full_for_dve, 1)
                all_read("act")
                for c in range(CHUNKS - 1):
                    for g in range(2):
                        pe.wait_ge(operand_ready, me.nth(operand_ready))
                        claim(1 + g, "dve")
                        mm(banks[1 + g][:, :], b_tok[:, g * CHUNKS + c, :], xs_dec[:, (2 * c + g) % 2, :],
                           True, True).then_inc(full_for_dve, 1)

                def broadcast_sums(hh):
                    b = hh % 2
                    claim(b, None)
                    one = const[FD, C_IDENT + 32 + hh:C_IDENT + 33 + hh]
                    mm(banks[b][:, :], one.to_broadcast([16, P]), acs[FD, :], True, True).then_inc(full_for_act, 1)

                broadcast_sums(0)
                for hh in range(HEADS):
                    if hh + 1 < HEADS:
                        broadcast_sums(hh + 1)
                    pe.wait_ge(operand_ready, me.nth(operand_ready))
                    b = 4 + hh // 2 % 2
                    if hh % 2 == 0:
                        claim(b, "dve")
                    rows = slice(hh % 2 * 64, hh % 2 * 64 + 64)
                    for c in range(CHUNKS):
                        cs, hs = slice(c * P, (c + 1) * P), slice(hh * 64, hh * 64 + 64)
                        ins = mm(banks[b][rows, cs], xs_tok[:, c, hs], m_dec[:, hh % 2, cs], True, c == 0)
                        if c > 0:
                            ins = mm(banks[b][rows, cs], prev[:, c - 1, hs], c_off[:, hh % 2, cs], False, True)
                    if hh % 2:
                        ins.then_inc(full_for_dve, 1)
                    else:
                        ins.then_inc(head_done, 1)
                sum_squares(6, hk, T)
                pe.wait_ge(operand_ready, me.nth(operand_ready))
                for n in range(KT):
                    project(n % 4, lambda k: y[:, k, :], T, "dve", pieces=2)
                hm = lambda k: h[:, k, T:ALL]
                sum_squares(4, hm, MEM)
                sum_squares(5, hk, T)
                pe.wait_ge(operand_ready, me.nth(operand_ready))
                for n in range(KT):
                    project(n % 4, hm, MEM)
                for n in range(KT):
                    project_tokens(n % 4, lambda k, j: h[:, k, T + j * P:T + (j + 1) * P], 2)
                for n in range(KT):
                    project(n % 4, hk, T)
                all_read("act")
                attention(mem_units())
                pe.wait_ge(operand_ready, me.nth(operand_ready))
                for n in range(KT):
                    project(n % 4, lambda k: y[:, k, :], T, "dve")

            pe.wait_ge(inputs_in, 16 * 4)
            for l in range(DEPTH):
                first_layer(l)
            pe_second(pe, me, claim, all_read, mm, weights, project, project_tokens, sum_squares, attention, unit)

        @block.scalar
        def _(act):
            me = Engine(act, act_step)
            A = nc.scalar.activation

            def bank_full():
                act.wait_ge(full_for_act, me.nth(full_for_act))

            def evacuate(o, i, func=ACT.Copy, **kw):
                bank_full()
                me.link(A(o, i, func, **kw), freed_by_act, wait=False)

            def squares(dst, src, n=KT):
                for k in range(0, n, 2):
                    me.link(A(dst[:, k:k + 2, :], src[:, k:k + 2, :], ACT.Square), squares_ready, wait=False)

            def roots(o):
                act.wait_ge(variance_ready, me.nth(variance_ready))
                me.link(A(o, o, ACT.Sqrt), root_ready, wait=False)

            def attention(units, project_out=None, n_beside=0, per=1):
                us = list(units)
                for i in range(len(us) + 1):
                    if i < len(us):
                        u = us[i]
                        act.wait_ge(max_ready, me.nth(max_ready))
                        at, j = i % 2 * ALL, i % 4
                        if u["sink"] is not None:
                            A(sinkp[:, j:j + 1], par1(u["l"], A_SINK + u["sink"]), ACT.Exp, bias=nmax[:, j:j + 1])
                        src = prob[:, at:at + u["nk"]] if u.get("bias") else banks[i % 2][:, 0:u["nk"]]
                        me.link(A(prob[:, at:at + u["nk"]], src, ACT.Exp, bias=nmax[:, j:j + 1],
                                  accum_out=rsum[:, j:j + 1]), exp_ready, wait=False)
                    if i >= 1:
                        u = us[i - 1]
                        nb = u["nk"] // P
                        for c in range(0, nb, 4):
                            b = 4 + (i - 1 + c // 4) % 2 if nb <= 4 else 4 + c // 4
                            m = min(4, nb - c)
                            at = (i - 1) % 2 * ALL + c * P
                            evacuate(probT[:, at:at + m * P], banks[b][:, 0:m * P])
                    if (i + 1) % per == 0 and (i + 1) // per <= n_beside:
                        project_out((i + 1) // per - 1)
                for n in range((len(us) + 1) // per, n_beside):
                    project_out(n)

            def fox_inputs(l, n):
                bank = banks[2 + n % 2]
                if n == 0:
                    bank_full()
                    me.link(A(gates[0:48, :], bank[0:48, :], ACT.Identity, bias=par1(l, A_GATE, rows=slice(0, 48))), freed_by_act)
                    me.link(A(gtmp[0:48, :], gates[0:48, :], ACT.Abs))
                    me.link(A(gtmp[0:48, :], gtmp[0:48, :], ACT.Exp, scale=-1.0))
                    me.link(A(a_neg, par1(l, A_ALOG, rows=FD), ACT.Exp))
                    me.link(A(gtmp[0:48, :], gtmp[0:48, :], ACT.Ln, bias=1.0), act_output, wait=False)
                elif n < 5:
                    evacuate(flat(3072 + (n - 1) * T, T), bank[:, :], scale=HD ** -0.5)
                elif n < 9:
                    evacuate(flat(5120 + (n - 5) * T, T), bank[:, :])
                elif n < 13:
                    evacuate(tiles(7168, 4, T)[:, :, (n - 9) * P:(n - 8) * P],
                             bank[:, :].rearrange("p (j n) -> p j n", j=4))
                else:
                    evacuate(y[:, n - 9, :], bank[:, :], ACT.Silu)

            def first_layer(l):
                if l:
                    act.wait_ge(act_input, me.nth(act_input))
                squares(h[:, :, 0:T], x[:, :, 0:T])
                roots(rstd[:, 0:T])
                for n in range(10):
                    if n < 4:
                        evacuate(flat(n * T, T), banks[n % 4][:, :], scale=HD ** -0.5)
                    elif n < 6:
                        evacuate(flat(2048 + (n - 4) * T, T), banks[n % 4][:, :])
                    else:
                        evacuate(y[:, n - 6, :], banks[n % 4][:, :], ACT.Silu)
                attention(swa_units(l), lambda n: fox_inputs(l, n), 17, 2)
                attention(fox_units(), lambda n: evacuate(y[:, 8 + n, :], banks[2 + n % 2][:, :], ACT.Silu), 8, 4)

                def convolved(n):
                    act.wait_ge(act_input, me.nth(act_input))
                    me.link(A(xbc[:, n, :], prob[:, n % 2 * ALL:n % 2 * ALL + T], ACT.Silu,
                              bias=par1(l, A_CONVB + n)), act_output, wait=False)

                for n in range(12):
                    bank_full()
                    if n == 0:
                        act.wait_ge(act_input, me.nth(act_input))
                    at = n % 2 * (T + 4) + 3
                    me.link(A(cpad[:, at:at + T], banks[n % 4][:, :], ACT.Copy), raw_ready, wait=False)
                    if n:
                        convolved(n - 1)
                convolved(11)
                for c in range(CHUNKS):
                    for g in range(2):
                        evacuate(xs_tok[:, c, g * T:(g + 1) * T], banks[(2 * c + g) % 4][:, :])
                for g in range(2):
                    evacuate(b_tok[:, g * 4:g * 4 + 4, :], banks[g][:, :].rearrange("p (c n) -> p c n", c=4))
                act.wait_ge(act_input, me.nth(act_input))
                me.link(A(small[:, 192:320], small[:, 192:320], ACT.Exp), act_output, wait=False)
                for hh in range(HEADS):
                    bank_full()
                    me.link(A(e_off[:, hh % 2, :], banks[hh % 2][:, :], ACT.Exp), act_output, wait=False)
                    act.wait_ge(act_input, me.nth(act_input))
                    me.link(A(diff[:, hh % 2, :], diff[:, hh % 2, :], ACT.Exp), act_output, wait=False)
                act.wait_ge(act_input, me.nth(act_input))
                squares(h[:, :, 0:T], y[:, 8:16, :])
                roots(rstd[:, 0:T])
                act.wait_ge(act_input, me.nth(act_input))
                squares(h[:, :, T:ALL], x[:, :, T:ALL])
                squares(h[:, :, 0:T], x[:, :, 0:T])
                roots(rstd[:, T:ALL])
                roots(rstd[:, 0:T])
                for n in range(8):
                    evacuate(flat(4096 + n * MEM, MEM), banks[n % 4][:, 0:MEM])
                for n in range(8):
                    evacuate(tiles(6144, 2, D_MODEL)[:, :, n * P:(n + 1) * P],
                             banks[n % 4][:, 0:MEM].rearrange("p (j n) -> p j n", j=2))
                for n in range(8):
                    evacuate(flat(n * T, T), banks[n % 4][:, :], scale=(D_MODEL // 4) ** -0.5)
                attention(mem_units())

            act.wait_ge(inputs_in, 16 * 4)
            for l in range(DEPTH):
                first_layer(l)
            act_second(act, me, A, bank_full, evacuate, squares, roots, attention)

        @block.vector
        def _(dve):
            me = Engine(dve, dve_step)
            V = nc.vector

            def bank_full():
                dve.wait_ge(full_for_dve, me.nth(full_for_dve))

            def await_(s):
                dve.wait_ge(s, me.nth(s))

            def inverse_deviation(b, r, n_features=D_MODEL):
                bank_full()
                me.link(V.tensor_scalar(rstd[:, r], banks[b][:, 0:r.stop - r.start], 1.0 / n_features, EPS,
                                        ALU.mult, ALU.add), variance_ready, wait=False)
                await_(root_ready)
                me.link(V.reciprocal(rstd[:, r], rstd[:, r]))

            def norm(b, dst, src, weight, r, n=KT):
                inverse_deviation(b, r)
                for k in range(n):
                    me.link(V.scalar_tensor_tensor(out=dst[:, k, :], in0=src[:, k, :], scalar=weight(k),
                                                   in1=rstd[:, r], op0=ALU.mult, op1=ALU.mult), wait=k == n - 1)

            def bias_scores(u, i):
                at = i % 2 * ALL
                if u["local"] is not None:
                    me.link(V.scalar_tensor_tensor(out=prob[:, at:at + T].rearrange("p (r c) -> p r c", r=8),
                                                   in0=banks[i % 2][:, :].rearrange("p (r c) -> p r c", r=8),
                                                   scalar=HD ** -0.5, in1=u["local"], op0=ALU.mult, op1=ALU.add),
                            freed_by_dve)
                    at += T
                me.link(V.tensor_scalar(prob[:, at:at + CTX], banks[2 + i % 2][:, 0:CTX], HD ** -0.5, None,
                                        ALU.mult), freed_by_dve)

            def attention(units):
                us = list(units)
                for i in range(len(us) + 2):
                    if i < len(us):
                        u, j = us[i], i % 4
                        bank_full()
                        m = nmax[:, j:j + 1]
                        if u.get("bias"):
                            bias_scores(u, i)
                            me.link(V.reduce_max(m, prob[:, i % 2 * ALL:i % 2 * ALL + u["nk"]], AX.X, negate=True),
                                    max_ready, wait=False)
                        elif u["sink"] is None:
                            me.link(V.reduce_max(m, banks[i % 2][:, 0:u["nk"]], AX.X, negate=True),
                                    max_ready, wait=False)
                        else:
                            me.link(V.reduce_max(m, banks[i % 2][:, 0:u["nk"]], AX.X, negate=True))
                            me.link(V.tensor_scalar(m, par1(u["l"], A_SINK + u["sink"]), -1.0, m, ALU.mult, ALU.min),
                                    max_ready, wait=False)
                    if 1 <= i <= len(us):
                        u, j = us[i - 1], (i - 1) % 4
                        await_(exp_ready)
                        s, r = rsum[:, j:j + 1], rinv[:, j:j + 1]
                        if u["sink"] is not None:
                            me.link(V.tensor_tensor(s, s, sinkp[:, j:j + 1], ALU.add))
                        me.link(V.reciprocal(r, s))
                        at = (i - 1) % 2 * ALL
                        p = prob[:, at:at + u["nk"]]
                        me.link(V.tensor_scalar(p, p, r, None, ALU.mult), prob_ready, wait=False)
                    if i >= 2 and us[i - 2]["closes"]:
                        u = us[i - 2]
                        bank_full()
                        for j in range(len(u["outs"])):
                            b = 6 + (me.awaited.get("outs", 0) + j) % 2
                            if u["gate"] is not None:
                                me.link(V.tensor_tensor(y[:, u["gate"], :], banks[b][:, :], y[:, u["gate"], :],
                                                        ALU.mult), freed_by_dve)
                            else:
                                d = u["dest"][j]
                                me.link(V.tensor_copy(d, banks[b][:, 0:d.shape[-1]]), freed_by_dve)
                        me.awaited["outs"] = me.awaited.get("outs", 0) + len(u["outs"])
                me.awaited["outs"] = 0

            def first_layer(l):
                norm(0, h[:, :, 0:T], x[:, :, 0:T], lambda k: par1(l, A_MIX + k), slice(0, T))
                me.notify(operand_ready)
                cos, sin = cst(C_TAB, T), cst(C_TAB + T, T)
                for n in range(5):
                    at = flat(n * T if n < 4 else 2048, T)
                    bank_full()
                    me.link(V.tensor_tensor(gtmp, banks[n % 4][:, :], sin, ALU.mult), freed_by_dve)
                    me.link(V.tensor_tensor(at, at, cos, ALU.mult))
                    me.link(V.tensor_tensor(at, at, gtmp, ALU.add))
                me.notify(operand_ready)
                attention(swa_units(l))
                await_(act_output)
                me.link(V.scalar_tensor_tensor(out=gates[0:8, :], in0=gates[0:8, :], scalar=0.0, in1=gtmp[0:8, :],
                                               op0=ALU.min, op1=ALU.subtract))
                me.link(V.scalar_tensor_tensor(out=gates[FD, :], in0=gates[FD, :], scalar=0.0, in1=gtmp[FD, :],
                                               op0=ALU.max, op1=ALU.add))
                c, negc = flat(9216, T), flat(9728, T)
                me.link(V.tensor_tensor_scan(c[0:8, :], gates[0:8, :], gates[0:8, :], 0.0, ALU.add, ALU.bypass))
                me.link(V.tensor_scalar(negc[0:8, :], c[0:8, :], -1.0, None, ALU.mult))
                me.link(V.tensor_scalar(a_neg, a_neg, -1.0, None, ALU.mult))
                me.link(V.tensor_scalar(gtmp[FD, :], gates[FD, :], a_neg, None, ALU.mult))
                for n in range(CHUNKS):
                    cs = slice(n * P, (n + 1) * P)
                    me.link(V.tensor_tensor_scan(acs[FD, cs], gtmp[FD, cs], gtmp[FD, cs], 0.0, ALU.add, ALU.bypass))
                me.notify(operand_ready)
                attention(fox_units())
                for r in range(2):
                    me.link(V.memset(cpad[:, r * (T + 4):r * (T + 4) + 3], 0.0))
                me.notify(act_input)
                for n in range(12):
                    await_(raw_ready)
                    if n >= 2:
                        await_(act_output)
                    acc = prob[:, n % 2 * ALL:n % 2 * ALL + T]
                    at = n % 2 * (T + 4)
                    me.link(V.tensor_scalar(acc, cpad[:, at:at + T], par1(l, A_CONV + 4 * n), None, ALU.mult))
                    for j in range(1, 4):
                        me.link(V.scalar_tensor_tensor(out=acc, in0=cpad[:, at + j:at + j + T],
                                                       scalar=par1(l, A_CONV + 4 * n + j), in1=acc,
                                                       op0=ALU.mult, op1=ALU.add), wait=j < 3,
                                s=act_input if j == 3 else None)
                await_(act_output)
                await_(act_output)
                me.notify(operand_ready)
                bank_full()
                me.link(V.tensor_copy(tok, banks[2][:, 0:192]), freed_by_dve)
                me.link(V.tensor_tensor(w_st, tok[:, 128:192], tok[:, 64:128], ALU.subtract))
                me.link(V.tensor_copy(chunk_decay, tok[:, 128:192]), act_input, wait=False)
                lower = cst(C_LOWER).rearrange("p (a n) -> p a n", a=1).to_broadcast([P, 4, P])
                for g in range(2):
                    bank_full()
                    me.link(V.tensor_tensor(cbm[:, g, :].rearrange("p (c n) -> p c n", c=4),
                                            banks[(0, 3)[g]][:, :].rearrange("p (c n) -> p c n", c=4), lower,
                                            ALU.mult), freed_by_dve)
                await_(act_output)
                me.link(V.tensor_tensor(w_st, w_st, tok[:, 0:64], ALU.mult))

                def per_head(v, c, g):
                    s = v[:, c * 16 + g * 8:c * 16 + g * 8 + 8]
                    return s.rearrange("p (e a) -> p e a", a=1).to_broadcast([P, 8, HD])

                def by_head(v):
                    return v.rearrange("p (e d) -> p e d", e=8)

                def decayed(n):
                    c, g = n // 2, n % 2
                    me.link(V.tensor_tensor(by_head(xs_dec[:, n % 2, :]), by_head(xs_tok[:, c, g * T:(g + 1) * T]),
                                            per_head(w_st, c, g), ALU.mult), operand_ready, wait=False)

                decayed(0)
                decayed(1)
                for n in range(6):
                    c, g = n // 2, n % 2
                    bank_full()
                    s = prev[:, c, g * T:(g + 1) * T]
                    if c == 0:
                        me.link(V.tensor_copy(s, banks[1 + g][:, :]), freed_by_dve)
                    else:
                        me.link(V.tensor_tensor(by_head(s), by_head(prev[:, c - 1, g * T:(g + 1) * T]),
                                                per_head(chunk_decay, c, g), ALU.mult))
                        me.link(V.tensor_tensor(s, s, banks[1 + g][:, :], ALU.add), freed_by_dve)
                    if n + 2 < 6:
                        decayed(n + 2)

                def pair_out(t):
                    bank_full()
                    me.link(V.scalar_tensor_tensor(out=gtmp, in0=xbc[:, t, :], scalar=par1(l, A_SKIP + t),
                                                   in1=banks[4 + t % 2][:, :], op0=ALU.mult, op1=ALU.add), freed_by_dve)
                    me.link(V.tensor_tensor(y[:, 8 + t, :], y[:, 8 + t, :], gtmp, ALU.mult))

                for hh in range(HEADS):
                    r, g = hh % 2, hh // 8
                    await_(act_output)
                    for c in range(CHUNKS):
                        cs = slice(c * P, (c + 1) * P)
                        me.link(V.tensor_scalar(diff[:, r, cs], banks[r][:, cs], tok[:, 64 + c * 16 + hh:65 + c * 16 + hh],
                                                0.0, ALU.subtract, ALU.min), act_input if c == 3 else None, wait=False)
                    if hh >= 3 and hh % 2:
                        pair_out((hh - 3) // 2)
                    if hh >= 2 and hh % 2 == 0:
                        await_(head_done)
                    await_(act_output)
                    for c in range(CHUNKS):
                        cs = slice(c * P, (c + 1) * P)
                        me.link(V.scalar_tensor_tensor(out=m_dec[:, r, cs], in0=diff[:, r, cs],
                                                       scalar=tok[:, c * 16 + hh:c * 16 + hh + 1], in1=cbm[:, g, cs],
                                                       op0=ALU.mult, op1=ALU.mult), wait=False)
                    me.link(V.tensor_tensor(c_off[:, r, :], xbc[:, 10 + g, :], e_off[:, r, :], ALU.mult),
                            operand_ready)
                await_(head_done)
                pair_out(7)
                me.notify(act_input)
                norm(6, y[:, 8:16, :], y[:, 8:16, :], lambda k: par1(l, A_SSM + k), slice(0, T))
                me.notify(operand_ready)
                for n in range(KT):
                    bank_full()
                    me.link(V.tensor_tensor(x[:, n, 0:T], x[:, n, 0:T], banks[n % 4][:, :], ALU.add), freed_by_dve)
                me.notify(act_input)
                norm(4, h[:, :, T:ALL], x[:, :, T:ALL], lambda k: par1(l, A_MEM + k), slice(T, ALL))
                me.notify(memory_read)
                norm(5, h[:, :, 0:T], x[:, :, 0:T], lambda k: par1(l, A_XQ + k), slice(0, T))
                me.notify(operand_ready)
                attention([dict(u, dest=[y[:, t, :] for t in u["dest"]]) for u in mem_units()])
                me.notify(operand_ready)
                for n in range(KT):
                    bank_full()
                    me.link(V.tensor_tensor(x[:, n, 0:T], x[:, n, 0:T], banks[n % 4][:, :], ALU.add), freed_by_dve)
                me.notify(act_input)

            dve.wait_ge(inputs_in, 16 * 4)
            for l in range(DEPTH):
                first_layer(l)
            dve_second(dve, me, V, bank_full, await_, inverse_deviation, norm, attention)
        stack.close()


def constants():
    f = np.float32
    c = np.zeros((P, N_CONST), f)
    i, j = np.arange(P)[:, None], np.arange(P)[None, :]
    c[:, C_IDENT:C_IDENT + P] = i == j
    c[:, C_ONES:C_ONES + P] = 1
    c[:, C_HEADS:C_HEADS + P] = i // HD == j // HD
    half = HD // 2
    same = i // HD == j // HD
    c[:, C_ROT1:C_ROT1 + P] = np.where(same & (i % HD == j % HD + half), -1, 0) + np.where(
        same & (i % HD == j % HD - half), 1, 0)
    quarter = HD // 4
    pair = i // half == j // half
    c[:, C_ROT2:C_ROT2 + P] = np.where(pair & (i % half == j % half + quarter), -1, 0) + np.where(
        pair & (i % half == j % half - quarter), 1, 0)
    c[:, C_CAUSAL:C_CAUSAL + P] = np.where(j <= i, 0, NEG)
    c[:, C_PREV:C_PREV + P] = np.where(j > i, 0, NEG)
    c[:, C_LOWER:C_LOWER + P] = j >= i
    for n, m in enumerate(LEVELS):
        ok = (i // (2 * m) == j // (2 * m)) & (i // m % 2 == 0) & (j // m % 2 == 1)
        c[:, C_LEVEL + n * P:C_LEVEL + (n + 1) * P] = ok
        c[:, C_LEVEL_BACK + n * P:C_LEVEL_BACK + (n + 1) * P] = ok.T
    c[:, C_LEVEL + 7 * P:C_LEVEL + 8 * P] = i == j
    c[:, C_LEVEL_BACK + 7 * P:C_LEVEL_BACK + 8 * P] = i == j
    cols = np.arange(P) % GRID
    start = np.clip(cols - NA_COLS // 2, 0, GRID - NA_COLS)[:, None]
    kc = np.arange(GRID)[None, :]
    c[:, C_COLMASK:C_COLMASK + GRID] = np.where((kc >= start) & (kc < start + NA_COLS), 0, NEG)
    c[:, C_SLOT] = np.arange(P) % CAP + 1
    c[:, C_SLOT + 1] = np.arange(P) % CAP_CTX + 1
    c[:, C_SLOTROW:C_SLOTROW + CAP] = np.arange(1, CAP + 1)
    d = np.arange(P) % HD
    inv = (1.0 / (f(10000.0) ** (np.arange(0, HD, 2, dtype=f) / f(HD)))).astype(f)
    ang = (np.arange(SEQ, dtype=f)[None, :] * inv[d % half][:, None]).astype(f)
    c[:, C_TAB:C_TAB + SEQ] = np.cos(ang)
    c[:, C_TAB + SEQ:C_TAB + 2 * SEQ] = np.sin(ang)
    return c


def second_tables():
    f = np.float32
    half, quarter = HD // 2, HD // 4
    d = np.arange(P) % HD
    t = np.arange(SEQ)
    inv = (f(10000.0) ** (-np.arange(quarter, dtype=f) / f(quarter))).astype(f)
    pos = np.where((d < half)[:, None], (t // GRID)[None, :], (t % GRID)[None, :]).astype(f)
    ang = (pos * inv[d % quarter][:, None]).astype(f)
    c = np.zeros((P, 2 * ALL), f)
    c[:, 0:SEQ] = np.cos(ang)
    c[:, SEQ:ALL] = 1
    c[:, ALL:ALL + SEQ] = np.sin(ang)
    return c


def columns(v):
    return v.reshape(-1, P).T


def parameters(a):
    out = np.zeros((P, DEPTH * (N_PAR1 + N_PAR2)), np.float32)
    for l in range(DEPTH):
        p = out[:, l * N_PAR1:(l + 1) * N_PAR1]
        p[:, A_MIX:A_MIX + 8] = columns(a["norm_mix_w"][l])
        p[:, A_XQ:A_XQ + 8] = columns(a["norm_xq_w"][l])
        p[:, A_MEM:A_MEM + 8] = columns(a["norm_mem_w"][l])
        p[:, A_SSM:A_SSM + 8] = columns(a["ssm_norm_w"][l])
        p[:, A_CONV:A_CONV + 48] = a["conv_w"][l].reshape(4, 12, P).transpose(2, 1, 0).reshape(P, 48)
        p[:, A_CONVB:A_CONVB + 12] = columns(a["conv_b"][l])
        p[:, A_SKIP:A_SKIP + 8] = columns(np.repeat(a["d_skip"][l], HD))
        p[:, A_SINK:A_SINK + 8] = a["swa_sinks"][l][None, :]
        p[0:8, A_GATE] = a["b_forget"][l]
        p[32:48, A_GATE] = a["dt_bias"][l]
        p[32:48, A_ALOG] = a["a_log"][l]
        p[:, A_FINAL:A_FINAL + 8] = columns(a["final_norm_w"])
        base = DEPTH * N_PAR1 + l * N_PAR2
        p = out[:, base:base + N_PAR2]
        p[:, B_MOD:B_MOD + 48] = columns(a["b_mod_2"][l])
        p[:, B_N1:B_N1 + 8] = columns(a["norm1_w_2"][l])
        p[:, B_N2:B_N2 + 8] = columns(a["norm2_w_2"][l])
        p[:, B_QN] = np.tile(a["na_q_norm_2"][l], 2)
        p[:, B_KN] = np.tile(a["na_k_norm_2"][l], 2)
        p[:, B_HGN] = np.tile(a["hg_norm_2"][l], 2)
        p[:, B_LB:B_LB + 12] = a["hg_lb_logits_2"].reshape(12, P).T
        p[:, B_CONV:B_CONV + 6] = a["conv_w_2"][l].reshape(3, 2, P).transpose(2, 1, 0).reshape(P, 6)
        p[:, B_COND:B_COND + 16:2] = columns(a["c_2"][0])
        p[:, B_COND + 1:B_COND + 16:2] = columns(a["c_ctx_2"])
    return out


def units_of(w):
    k, n = w.shape[0] // (KT * P), w.shape[1] // P
    return w.reshape(k, KT, P, n, P).transpose(3, 0, 2, 1, 4).reshape(n * k, P, KT * P)


def first_stream(a, l):
    w = a["w_in"][l]
    at = np.cumsum([0, 512, 128, 128, 512, 512, 512, 512, 8, 512, 1024, 1536, 16])
    q_a, k_a, v_a, g_a, q_b, k_b, v_b, f_b, g_b, z, xbc, dt = (w[:, at[i]:at[i + 1]] for i in range(12))

    def paired(m):
        return m.reshape(-1, 2, 4, HD).transpose(0, 2, 1, 3).reshape(-1, 512)

    narrow = np.zeros((D_MODEL, P), w.dtype)
    narrow[:, 0:8] = f_b
    narrow[:, 32:48] = dt
    wo = a["w_out"][l].copy()
    wo[0:512] = a["w_out"][l][0:512].reshape(2, 4, HD, -1).transpose(1, 0, 2, 3).reshape(512, -1)
    cols = np.concatenate([paired(q_a), k_a, v_a, paired(g_a), narrow, q_b, k_b, v_b, g_b, z, xbc], axis=1)
    return [units_of(cols), units_of(wo)] + [units_of(a[n][l]) for n in ("w_mk", "w_mv", "w_mq", "w_mo")]


def second_stream(a, l):
    w = a["w_in_2"][l]
    at = np.cumsum([0] + [384] * 8 + [256] * 3)
    q, k, v, hq, hf, hb, hi, hgate, b, c, u = (w[:, at[i]:at[i + 1]] for i in range(11))
    out = [units_of(a["w_mod_2"][l]), units_of(np.concatenate([c, u, b, q, k, v, hq, hf, hb, hi, hgate], axis=1)),
           units_of(a["w_out_2"][l])]
    router = np.zeros((D_MODEL, P), w.dtype)
    router[:, 0:N_EXPERTS] = a["w_router_2"][l]
    out.append(units_of(router))
    for e in range(N_EXPERTS):
        out += [units_of(a["w_exp_gate_2"][l, e]), units_of(a["w_exp_up_2"][l, e])]
        out.append(a["w_exp_down_2"][l, e].reshape(4, P, 4, 256).transpose(2, 1, 0, 3).reshape(4, P, 1024))
    return out


def bias_windows(rpb):
    wide = np.zeros((NA_HEADS, RPB_ROWS + 1, 2 * GRID), rpb.dtype)
    wide[:, 1:, 48:48 + 31] = rpb
    at = (GRID - 1) - np.arange(GRID)[:, None] + np.arange(GRID)[None, :]
    win = wide[:, :, at]
    halves = [win[:, 2:16], win[:, 1:15]]
    return np.concatenate([m.transpose(2, 0, 1, 3).reshape(GRID, -1) for m in halves])


def layout(inputs):
    a = {k: np.asarray(v) for k, v in inputs.items()}
    stream = []
    for l in range(DEPTH):
        stream += first_stream(a, l)
    for l in range(DEPTH):
        stream += second_stream(a, l)
    return {
        "consts": constants(),
        "params": parameters(a),
        "xT": np.ascontiguousarray(a["x"][0].T),
        "memT": np.ascontiguousarray(a["mem"][0].T),
        "ctxT": np.ascontiguousarray(a["ctx_2"][0].T),
        "tables2": second_tables(),
        "bias": np.stack([bias_windows(a["na_rpb_2"][l]) for l in range(DEPTH)]),
        "stream": np.concatenate(stream),
    }


def kernel(**inputs):
    from concourse import bacc
    from concourse.bass_utils import run_bass_kernel_spmd

    nc = bacc.Bacc("TRN2", target_bir_lowering=False, num_devices=1)
    arrays = {f"in_{n}": v for n, v in layout(inputs).items()}
    places = {n[3:]: nc.dram_tensor(n, v.shape, mybir.dt.float32, kind="ExternalInput").ap()
              for n, v in arrays.items()}
    out = nc.dram_tensor("out", (D_MODEL, SEQ), mybir.dt.float32, kind="ExternalOutput").ap()
    build(nc, places, out)
    r = run_bass_kernel_spmd(nc, [arrays], core_ids=[0])
    return np.ascontiguousarray(r.results[0]["out"].T)[None]
```
